# Optimizing a Trainium2 kernel written in Bass

```python
import jax, jax.numpy as jnp
from jax import lax
import numpy as np

D_MODEL = 1024
BATCH = 1
SEQ = 256
DEPTH = 2

MEM_LEN = 256
RET_HEADS = 4
RET_DK = 64
RET_DV = 128
RET_CHUNK = 128
GLA_HEADS = 4
GLA_DK = 64
GLA_DV = 128
GLA_CHUNK = 64
GLA_GATE_RANK = 16
GLA_GATE_TAU = 16.0
XA_HEADS = 4
XA_DH = D_MODEL // XA_HEADS
D_FF = 2816
ROPE_BASE = 10000.0
EPS = 1e-6

RET_W = RET_HEADS * RET_DV
GLA_W = GLA_HEADS * GLA_DV
MIX_W = RET_W + GLA_W
IN_SIZES = (
    RET_HEADS * RET_DK,
    RET_HEADS * RET_DK,
    RET_W,
    RET_W,
    GLA_HEADS * GLA_DK,
    GLA_HEADS * GLA_DK,
    GLA_W,
    GLA_GATE_RANK,
    GLA_W,
)
IN_DIM = sum(IN_SIZES)

kernel_name = "hybrid_retention_gla_macaron_block"

def _split_points():
    pts, acc = [], 0
    for s in IN_SIZES[:-1]:
        acc += s
        pts.append(acc)
    return pts

def rmsnorm(x, g):
    xf = x.astype(jnp.float32)
    y = xf * lax.rsqrt(jnp.mean(xf * xf, axis=-1, keepdims=True) + EPS)
    return (y * g.astype(jnp.float32)).astype(x.dtype)

def swiglu(h, w_gate, w_up, w_down):
    return (jax.nn.silu(h @ w_gate) * (h @ w_up)) @ w_down

def rope(x, cos, sin):
    half = x.shape[-1] // 2
    x1, x2 = x[..., :half], x[..., half:]
    c, s = cos.astype(x.dtype), sin.astype(x.dtype)
    return jnp.concatenate([x1 * c - x2 * s, x1 * s + x2 * c], axis=-1)

def to_chunks(x, c):
    b, t, h, d = x.shape
    return x.reshape(b, t // c, c, h, d).transpose(1, 0, 3, 2, 4)

def from_chunks(o):
    n, b, h, c, d = o.shape
    return o.transpose(1, 0, 3, 2, 4).reshape(b, n * c, h, d)

def retention(q, k, v):
    b, t, h, dk = q.shape
    dv = v.shape[-1]
    c = RET_CHUNK
    log_gamma = jnp.log1p(-jnp.exp2(-5.0 - jnp.arange(h, dtype=jnp.float32)))
    idx = jnp.arange(c, dtype=jnp.float32)
    rel = idx[:, None] - idx[None, :]
    causal = rel >= 0
    decay_in = jnp.where(causal[None], jnp.exp(jnp.where(causal, rel, 0.0)[None] * log_gamma[:, None, None]), 0.0)
    q_dec = jnp.exp((idx + 1.0)[None, :] * log_gamma[:, None])
    k_dec = jnp.exp((c - 1.0 - idx)[None, :] * log_gamma[:, None])
    chunk_dec = jnp.exp(c * log_gamma)

    def step(state, inp):
        qc, kc, vc = inp
        scores = jnp.einsum('bhid,bhjd->bhij', qc, kc) * decay_in[None]
        o = (jnp.einsum('bhij,bhjv->bhiv', scores, vc)
             + jnp.einsum('bhid,bhdv->bhiv', qc * q_dec[None, :, :, None], state))
        state = (chunk_dec[None, :, None, None] * state
                 + jnp.einsum('bhjd,bhjv->bhdv', kc * k_dec[None, :, :, None], vc))
        return state, o

    s0 = jnp.zeros((b, h, dk, dv), jnp.float32)
    _, o = lax.scan(step, s0, (to_chunks(q, c), to_chunks(k, c), to_chunks(v, c)))
    return from_chunks(o)

def gla(q, k, v, log_a):
    b, t, h, dk = q.shape
    dv = v.shape[-1]
    c = GLA_CHUNK
    mask = jnp.tril(jnp.ones((c, c), dtype=bool))[:, :, None]

    def step(state, inp):
        qc, kc, vc, gc = inp
        cum = jnp.cumsum(gc, axis=-2)
        diff = cum[:, :, :, None, :] - cum[:, :, None, :, :]
        decay = jnp.exp(jnp.where(mask, diff, -jnp.inf))
        scores = jnp.einsum('bhid,bhjd,bhijd->bhij', qc, kc, decay)
        o = (jnp.einsum('bhij,bhjv->bhiv', scores, vc)
             + jnp.einsum('bhid,bhdv->bhiv', qc * jnp.exp(cum), state))
        last = cum[:, :, -1:, :]
        state = (jnp.exp(last[:, :, 0, :])[..., None] * state
                 + jnp.einsum('bhjd,bhjv->bhdv', kc * jnp.exp(last - cum), vc))
        return state, o

    s0 = jnp.zeros((b, h, dk, dv), jnp.float32)
    _, o = lax.scan(step, s0, (to_chunks(q, c), to_chunks(k, c), to_chunks(v, c), to_chunks(log_a, c)))
    return from_chunks(o)

def hybrid_mixer(h, cos, sin, w_in, w_a2, b_a2, ret_norm_g, gla_norm_g, w_out):
    bsz, t, _ = h.shape
    z = h @ w_in
    rq, rk, rv, rg, gq, gk, gv, ga, gg = jnp.split(z, _split_points(), axis=-1)
    rq = rope(rq.reshape(bsz, t, RET_HEADS, RET_DK), cos, sin)
    rk = rope(rk.reshape(bsz, t, RET_HEADS, RET_DK), cos, sin) * (RET_DK ** -0.5)
    ro = retention(rq, rk, rv.reshape(bsz, t, RET_HEADS, RET_DV))
    ro = rmsnorm(ro, ret_norm_g).astype(h.dtype).reshape(bsz, t, RET_W) * jax.nn.silu(rg)
    log_a = jax.nn.log_sigmoid((ga @ w_a2 + b_a2).astype(jnp.float32)) / GLA_GATE_TAU
    log_a = log_a.reshape(bsz, t, GLA_HEADS, GLA_DK)
    go = gla(gq.reshape(bsz, t, GLA_HEADS, GLA_DK) * (GLA_DK ** -0.5),
             gk.reshape(bsz, t, GLA_HEADS, GLA_DK),
             gv.reshape(bsz, t, GLA_HEADS, GLA_DV), log_a)
    go = rmsnorm(go, gla_norm_g).astype(h.dtype).reshape(bsz, t, GLA_W) * jax.nn.silu(gg)
    return jnp.concatenate([ro, go], axis=-1) @ w_out

def memory_cross_attn(h, mem_n, w_q, w_kv, w_o):
    bsz, t, _ = h.shape
    m = mem_n.shape[1]
    q = (h @ w_q).reshape(bsz, t, XA_HEADS, XA_DH)
    k, v = jnp.split(mem_n @ w_kv, 2, axis=-1)
    k = k.reshape(bsz, m, XA_HEADS, XA_DH)
    v = v.reshape(bsz, m, XA_HEADS, XA_DH)
    s = jnp.einsum('bthd,bmhd->bhtm', q, k).astype(jnp.float32) * (XA_DH ** -0.5)
    p = jax.nn.softmax(s, axis=-1).astype(v.dtype)
    o = jnp.einsum('bhtm,bmhd->bthd', p, v).reshape(bsz, t, D_MODEL)
    return o @ w_o

def setup_inputs(seed: int = 0) -> dict:
    key = jax.random.key(seed)
    ks = iter(jax.random.split(key, 40))
    f32 = jnp.float32

    def w(shape, fan_in):
        return jax.random.normal(next(ks), (DEPTH,) + shape, f32) * (fan_in ** -0.5)

    def gain(shape):
        return 1.0 + 0.02 * jax.random.normal(next(ks), (DEPTH,) + shape, f32)

    x = jax.random.normal(next(ks), (BATCH, SEQ, D_MODEL), f32)
    mem = jax.random.normal(next(ks), (BATCH, MEM_LEN, D_MODEL), f32)
    offset = jax.random.randint(next(ks), (BATCH, 1), 0, 4096, dtype=jnp.int32)
    positions = offset + jnp.arange(SEQ, dtype=jnp.int32)[None, :]
    return {
        "x": x, "mem": mem, "positions": positions,
        "ffn1_pre_g": gain((D_MODEL,)),
        "ffn1_w_gate": w((D_MODEL, D_FF), D_MODEL),
        "ffn1_w_up": w((D_MODEL, D_FF), D_MODEL),
        "ffn1_w_down": w((D_FF, D_MODEL), D_FF),
        "ffn1_post_g": gain((D_MODEL,)),
        "mix_pre_g": gain((D_MODEL,)),
        "w_in": w((D_MODEL, IN_DIM), D_MODEL),
        "w_a2": w((GLA_GATE_RANK, GLA_HEADS * GLA_DK), GLA_GATE_RANK),
        "b_a2": 0.01 * jax.random.normal(next(ks), (DEPTH, GLA_HEADS * GLA_DK), f32),
        "ret_norm_g": gain((RET_HEADS, RET_DV)),
        "gla_norm_g": gain((GLA_HEADS, GLA_DV)),
        "w_out": w((MIX_W, D_MODEL), MIX_W),
        "mix_post_g": gain((D_MODEL,)),
        "xa_pre_g": gain((D_MODEL,)),
        "xa_mem_g": gain((D_MODEL,)),
        "xa_w_q": w((D_MODEL, D_MODEL), D_MODEL),
        "xa_w_kv": w((D_MODEL, 2 * D_MODEL), D_MODEL),
        "xa_w_o": w((D_MODEL, D_MODEL), D_MODEL),
        "xa_post_g": gain((D_MODEL,)),
        "ffn2_pre_g": gain((D_MODEL,)),
        "ffn2_w_gate": w((D_MODEL, D_FF), D_MODEL),
        "ffn2_w_up": w((D_MODEL, D_FF), D_MODEL),
        "ffn2_w_down": w((D_FF, D_MODEL), D_FF),
        "ffn2_post_g": gain((D_MODEL,)),
    }

def reference(x, mem, positions,
              ffn1_pre_g, ffn1_w_gate, ffn1_w_up, ffn1_w_down, ffn1_post_g,
              mix_pre_g, w_in, w_a2, b_a2, ret_norm_g, gla_norm_g, w_out, mix_post_g,
              xa_pre_g, xa_mem_g, xa_w_q, xa_w_kv, xa_w_o, xa_post_g,
              ffn2_pre_g, ffn2_w_gate, ffn2_w_up, ffn2_w_down, ffn2_post_g):
    inv_freq = ROPE_BASE ** (-jnp.arange(0, RET_DK, 2, dtype=jnp.float32) / RET_DK)
    ang = positions.astype(jnp.float32)[..., None] * inv_freq
    cos = jnp.cos(ang)[:, :, None, :]
    sin = jnp.sin(ang)[:, :, None, :]

    for l in range(DEPTH):
        x = x + 0.5 * rmsnorm(swiglu(rmsnorm(x, ffn1_pre_g[l]), ffn1_w_gate[l], ffn1_w_up[l], ffn1_w_down[l]), ffn1_post_g[l])
        x = x + rmsnorm(hybrid_mixer(rmsnorm(x, mix_pre_g[l]), cos, sin, w_in[l], w_a2[l], b_a2[l],
                                     ret_norm_g[l], gla_norm_g[l], w_out[l]), mix_post_g[l])
        x = x + rmsnorm(memory_cross_attn(rmsnorm(x, xa_pre_g[l]), rmsnorm(mem, xa_mem_g[l]),
                                          xa_w_q[l], xa_w_kv[l], xa_w_o[l]), xa_post_g[l])
        x = x + 0.5 * rmsnorm(swiglu(rmsnorm(x, ffn2_pre_g[l]), ffn2_w_gate[l], ffn2_w_up[l], ffn2_w_down[l]), ffn2_post_g[l])
    return x


_drawn_inputs = setup_inputs


def setup_inputs(seed=0):
    import zlib

    import numpy as np

    out = dict(_drawn_inputs(seed))
    spreads = {}
    factors = {'ffn1_post_g': 2.715,
     'b_a2': 8.0,
     'ret_norm_g': 3.924,
     'gla_norm_g': 3.749,
     'xa_pre_g': 3.251,
     'xa_post_g': 2.999,
     'ffn2_pre_g': 4.783,
     'ffn2_post_g': 6.955}
    for name, (base, spread) in spreads.items():
        noise = np.random.default_rng([zlib.crc32(name.encode()), seed]).standard_normal(out[name].shape)
        drawn = base * np.exp(spread * noise) if base else spread * noise
        out[name] = __import__('jax').numpy.asarray(drawn.astype(out[name].dtype))
    for name, factor in factors.items():
        out[name] = (out[name] * factor).astype(out[name].dtype)
    return out
```

```python
from contextlib import ExitStack

import numpy as np

import concourse.bass as bass
from concourse import mybir

F32 = mybir.dt.float32
F32R = mybir.dt.float32r
BF16 = mybir.dt.bfloat16
I32 = mybir.dt.int32
I8 = mybir.dt.int8
ALU = mybir.AluOpType
ACT = mybir.ActivationFunctionType
AX = mybir.AxisListType
ds = bass.ds

P = 128
LAYERS = 2
D = 1024
TOK = 256
TT = TOK // P
KD = D // P
COL = 512
F = 2816
FU = F // (COL // 2)
KF = F // P
HEADS = 4
DK = 64
DV = 128
RANK = 16
XH = 4
EPS = 1e-6
TAU = 16.0

G_FFN1, G_MIX, G_MEM, G_XA, G_FFN2, G_HEAD = range(6)
N_GAINS = 6
DOWN = [(n, k, min(8, KF - k) // 2) for n in range(2) for k in range(0, KF, 8)]


def ffn_chunks(f):
    gain = (G_FFN1, G_FFN2)[f]
    up = [(f"gu{f}", j, 0, 4, gain) for j in range(FU)]
    return up + [(f"down{f}", n, k, nk, None) for n, k, nk in DOWN]


CHUNKS = ffn_chunks(0)
C_IN = len(CHUNKS)
CHUNKS += [("in", c, 0, 4, G_MIX) for c in range(6)]
C_OUT = len(CHUNKS)
CHUNKS += [("out", c, 0, 4, G_HEAD) for c in range(2)]
C_KV = len(CHUNKS)
CHUNKS += [("kv", c, 0, 4, G_MEM) for c in range(4)]
C_Q = len(CHUNKS)
CHUNKS += [("q", c, 0, 4, G_XA) for c in range(2)]
C_O = len(CHUNKS)
CHUNKS += [("o", c, 0, 4, None) for c in range(2)]
C_FFN2 = len(CHUNKS)
CHUNKS += ffn_chunks(1)
N_CH = len(CHUNKS)
C_FFN = (0, C_FFN2)
HALVES = 2 * N_CH
assert N_CH % 2 == 0

Q_IN = FU + 2
Q_OUT = Q_IN + 6
Q_KV = Q_OUT + 2
Q_Q = Q_KV + 4
Q_AV = Q_Q + 2
Q_O = Q_AV + 2
Q_FFN = (0, Q_O + 2)
N_Q = Q_FFN[1] + FU + 2
assert N_Q % 2 == 0
LAST_CHUNK = {Q_FFN[f] + j: C_FFN[f] + j for f in range(2) for j in range(FU)}
LAST_CHUNK.update({Q_FFN[f] + FU + n: C_FFN[f] + FU + 3 * n + 2 for f in range(2) for n in range(2)})
LAST_CHUNK.update({Q_IN + c: C_IN + c for c in range(6)})
for q0, c0, n in ((Q_OUT, C_OUT, 2), (Q_KV, C_KV, 4), (Q_Q, C_Q, 2), (Q_O, C_O, 2)):
    LAST_CHUNK.update({q0 + c: c0 + c for c in range(n)})
PASSES = 2 * N_CH + XH

XUSE = [(t, a) for t in range(TT) for a in range(2)]
T_USES = [("x", 0, 1, 0), ("x", 0, 1, 1)] + [("h", 0, j) for j in range(FU)]
T_USES += [("x", 1, t, a) for t, a in XUSE]
T_USES += [("ga", 0), ("ga", 1), ("gqk", 0), ("gqk", 1), ("rqk", 0), ("rqk", 1)]
T_USES += [("mix", t, a) for t, a in XUSE]
T_USES += [("mem", t, a) for t, a in XUSE]
T_USES += [("x", 2, t, a) for t, a in XUSE]
T_USES += [("p", h) for h in range(XH)]
T_USES += [("x", 3, t, a) for t, a in XUSE]
T_USES += [("h", 1, j) for j in range(FU)]
T_USES += [("x", 4, 0, 0), ("x", 4, 0, 1)]
N_T = len(T_USES)
assert N_T % 2 == 0
SPLIT_USES = [u for u in T_USES if u[0] in ("x", "h", "mix", "mem")]
N_TS = len(SPLIT_USES)

LEVELS = [128, 64, 32, 16, 8, 4, 2, 1]
M_USES = ["z", "diag", "lv0", "lv1", "rj0", "lv2", "rj1", "lv3", "lv4", "ro", "lv5", "lv6", "lv7", "go",
          "s0", "s1"]
N_M = len(M_USES)
POOL_STEPS = 50


def program(nc, a, out):
    ctx = ExitStack()
    with ctx:
        def sb(name, shape, dt=F32, stack=ctx):
            return stack.enter_context(nc.sbuf_tensor(name, shape, dt))

        def sem(name):
            return ctx.enter_context(nc.semaphore(name))

        raw = sb("raw", [P, 4, 4, COL])
        w_hi = sb("w_hi", [P, 4, 4, COL], F32R)
        w_lo = sb("w_lo", [P, 4, 4, COL], F32R)
        x = sb("x", [P, TT, D])
        xT_hi = sb("xT_hi", [P, KD, TOK], F32R)
        xT_lo = sb("xT_lo", [P, KD, TOK], F32R)
        yg = sb("yg", [P, TT, D])
        post_gain = sb("post_gain", [P, D])
        ident = sb("ident", [P, P])
        ones = sb("ones", [P, P])
        decay = sb("decay", [P, 2, 2, TOK])
        lv_words = sb("lv_words", [P, 7 * 64 // 4], I32)
        lv_mask = lv_words[:, :].bitcast(I8).rearrange("p (v i) -> p v i", v=7)
        rope_c = sb("rope_c", [P, TT, DK])
        rope_s = sb("rope_s", [P, TT, DK])
        gains = sb("gains", [P, LAYERS * N_GAINS * KD])
        w_a2 = sb("w_a2", [RANK, LAYERS, 256])
        w_a2_l = sb("w_a2_l", [RANK, 256])
        b_a2 = sb("b_a2", [P, LAYERS * 2])
        w_ga = sb("w_ga", [P, LAYERS, KD, RANK])
        w_ga_s = sb("w_ga_s", [P, KD, RANK])
        w_ga_hi = sb("w_ga_hi", [P, KD, RANK], F32R)
        w_ga_lo = sb("w_ga_lo", [P, KD, RANK], F32R)
        junk_y = sb("junk_y", [P, COL], BF16)
        junk_x = sb("junk_x", [P, D], BF16)
        half_neg = sb("half_neg", [P, 8])
        yss = sb("yss", [P, TT, 2])
        xss = sb("xss", [P, TT])
        v_post = sb("v_post", [P, TT])
        r_post = sb("r_post", [P, TT])
        v_pre = sb("v_pre", [P, TT])
        r_pre = sb("r_pre", [P, TT])
        r_half = sb("r_half", [P, TT])
        c_half = sb("c_half", [P, TT])
        r_8 = sb("r_8", [P, TT])
        r_16 = sb("r_16", [P, TT])
        n_16 = sb("n_16", [P, TT])
        hss = sb("hss", [P, TT, 8])
        v_head = sb("v_head", [P, TT, 8])
        r_head = sb("r_head", [P, TT, 8])
        f_head = sb("f_head", [P, TT, 8])
        mss = sb("mss", [P, TT])
        v_mem = sb("v_mem", [P, TT])
        r_mem = sb("r_mem", [P, TT])
        smax = sb("smax", [P, XH, TT])
        nbias = sb("nbias", [P, XH, TT])
        rsum = sb("rsum", [P, XH, TT])
        rinv = sb("rinv", [P, XH, TT])
        ga_tok = sb("ga_tok", [P, TT, RANK])
        gaT = sb("gaT", [RANK, TOK])

        with ExitStack() as region:
            hT_hi = sb("hT_hi", [P, KF, TOK], F32R, region)
            hT_lo = sb("hT_lo", [P, KF, TOK], F32R, region)
            h_tok = sb("h_tok", [P, 2, TT, 256], F32, region)
            th = sb("th", [P, TT, 256], F32, region)
            gt = sb("gt", [P, TT, 256], F32, region)
        with ExitStack() as region:
            o_sb = sb("o_sb", [P, TT, D], F32, region)
            gate = sb("gate", [P, TT, D], F32, region)
            v_tok = sb("v_tok", [P, TT, D], F32, region)
            gqk = sb("gqk", [P, TT, COL], F32, region)
            rqk = sb("rqk", [P, TT, COL], F32, region)
            gT = sb("gT", [P, 4, TOK], F32, region)
            rT = sb("rT", [P, 4, TOK], F32, region)
            pr0 = sb("pr0", [P, 2, 2, TOK], F32, region)
            pr1 = sb("pr1", [P, 2, 2, P], F32, region)
            pg = sb("pg", [P, 2, 4, P], F32, region)
            pgx = sb("pgx", [P, 2, 2, P], F32, region)
            rot_a = sb("rot_a", [P, COL], F32, region)
            rot_b = sb("rot_b", [P, COL], F32, region)
            cum = sb("cum", [P, 2, TOK], F32, region)
        zb = gate[:, 0, 0:COL].rearrange("p (r i) -> p r i", r=2)
        lg = gate[:, 0, COL:2 * COL].rearrange("p (r i) -> p r i", r=2)
        dec = [o_sb[:, n, COL:2 * COL] for n in range(2)]
        av = [gqk[:, n, :] for n in range(2)]

        with ExitStack() as region:
            kT = sb("kT", [P, KD, TOK], F32, region)
            vx = sb("vx", [P, TT, D], F32, region)
            mem_t = sb("mem_t", [P, TT, D], F32, region)
            mT_hi = sb("mT_hi", [P, KD, TOK], F32R, region)
            mT_lo = sb("mT_lo", [P, KD, TOK], F32R, region)
            qT = sb("qT", [P, KD, TOK], F32, region)
            pr = sb("pr", [P, 2, TT, TOK], F32, region)
            pT = sb("pT", [P, 2, TT, TOK], F32, region)
        with ExitStack() as region:
            pos_i = sb("pos_i", [P, TT], I32, region)
            pos_f = sb("pos_f", [P, TT], F32, region)
            inv_f = sb("inv_f", [P, 32], F32, region)
            ang = sb("ang", [P, TT, 32], F32, region)
            turns = sb("turns", [P, TT, 32], F32, region)
            rest = [sb(f"rest{i}", [P, TT, 32], F32, region) for i in range(4)]
            absr = sb("absr", [P, TT, 32], F32, region)
            carg = sb("carg", [P, TT, 32], F32, region)
            sin_t = sb("sin_t", [P, TT, 32], F32, region)
            cos_t = sb("cos_t", [P, TT, 32], F32, region)

        acc = [[ctx.enter_context(nc.psum_tensor(f"acc{s}{t}", [P, COL], F32)) for t in range(TT)] for s in range(2)]
        tb = [ctx.enter_context(nc.psum_tensor(f"tb{i}", [P, COL], F32)) for i in range(2)]
        mb = [ctx.enter_context(nc.psum_tensor(f"mb{i}", [P, COL], F32)) for i in range(2)]

        s_const = sem("const_loaded")
        s_x_in = [sem(f"x_loaded{t}") for t in range(TT)]
        s_first = sem("identity_and_gains_loaded")
        s_raw = [sem(f"raw_loaded{i}") for i in range(4)]
        s_gain = sem("post_gain_loaded")
        s_mem = sem("mem_loaded")
        s_out = sem("out_stored")
        s_hi = sem("w_hi_ready")
        s_lo = sem("w_lo_ready")
        s_half = sem("first_half_used")
        s_acc = sem("pass_done")
        s_accf = [sem(f"acc_free{i}") for i in range(4)]
        s_t = sem("transposed")
        s_thi = sem("transposed_hi_copied")
        s_tev = sem("transposed_evacuated")
        s_m = [sem(f"mixer_bank_done{i}") for i in range(2)]
        s_mf = [sem(f"mixer_bank_free{i}") for i in range(2)]
        s_ysq = sem("y_squared")
        s_xsq = sem("x_squared")
        s_rpost = sem("r_post_ready")
        s_rpre = sem("r_pre_ready")
        s_x = sem("x_ready")
        s_tanh = sem("tanh_ready")
        s_gated = sem("gate_scaled")
        s_pool = sem("pool_step")
        s_setup = sem("setup_step")
        s_trig = sem("sin_cos_ready")
        s_rope_t = sem("rope_table_ready")
        s_gas = sem("w_ga_scaled")
        s_gah = sem("w_ga_hi_ready")
        s_gal = sem("w_ga_lo_ready")
        s_a2 = sem("w_a2_ready")
        s_lsig = sem("log_sigmoid_step")
        s_la = sem("log_gate_ready")
        s_cum = sem("cum_ready")
        s_tmp = sem("exponent_ready")
        s_dec = sem("decay_ready")
        s_av = sem("decayed_qk_ready")
        s_rope = sem("rope_done")
        s_hss = sem("head_squares_summed")
        s_of = sem("heads_normed")
        s_gtanh = sem("mix_gate_tanh")
        s_mixed = sem("mixed_ready")
        s_msq = sem("mem_squared")
        s_rmem = sem("r_mem_ready")
        s_memn = sem("mem_normed")
        s_smax = sem("score_max_ready")
        s_nb = sem("exp_bias_ready")
        s_rinv = sem("row_sum_inverted")
        s_p = sem("probs_ready")
        s_ohi = sem("attention_hi_copied")

        def half_no(l, ci, h):
            return l * HALVES + 2 * ci + h

        def t_no(l, use):
            if use[0] == "x" and use[1:3] == (0, 0):
                return l * N_T + use[3]
            return l * N_T + T_USES.index(use) + 2

        def t_bank(use):
            return (use[3] if use[:3] == ("x", 0, 0) else T_USES.index(use)) % 2

        def ts_no(l, use):
            if use[0] == "x" and use[1:3] == (0, 0):
                return l * N_TS + use[3]
            return l * N_TS + SPLIT_USES.index(use) + 2

        def m_no(l, use):
            return l * N_M + M_USES.index(use)

        def chunk_pass_no(l, ci, t):
            return l * PASSES + 2 * ci + t + (XH if ci >= C_O else 0)

        def pass_no(l, q, t):
            if Q_AV <= q < Q_O:
                return l * PASSES + 2 * C_O + 2 * (q - Q_AV) + t
            return chunk_pass_no(l, LAST_CHUNK[q], t)

        def acc_uses(l, q):
            return l * (N_Q // 2) + q // 2

        def bank(q, t):
            return 2 * (q % 2) + t

        def other(l):
            return l * -1 + 1

        def weight_src(ci, h, l, j=None):
            lay = l
            if ci >= N_CH:
                ci, lay = ci - N_CH, other(l)
            name, col, k0, nk, _ = CHUNKS[ci]
            w = a[name]
            col = col if j is None else j
            n_cols = w.shape[1]
            flat = w.rearrange("l c p k -> (l c) p k")
            src = flat[ds(lay * n_cols + col, 1), :, (k0 + h * nk) * COL:(k0 + h * nk + nk) * COL]
            return src.rearrange("o p k -> (o p) k"), nk

        block = ctx.enter_context(nc.Block())

        @block.sync
        def _(sp):
            def load(l, ci, j=None, extra=0):
                for h in range(2):
                    slot = (2 * ci + h) % 4
                    src, nk = weight_src(ci, h, l, j)
                    if not isinstance(l, int):
                        sp.wait_ge(s_lo, half_no(l, ci, h) + extra - 3)
                    sp.dma_start(raw[:, slot, 0:nk, :].rearrange("p k n -> p (k n)"), src).then_inc(s_raw[slot], 16)

            def load_post_gain(l, phase):
                q_last = {0: Q_FFN[0] + FU + 1, 1: Q_OUT + 1, 2: Q_O + 1, 3: Q_FFN[1] + FU + 1}
                prev = q_last[(phase - 1) % 4]
                sp.wait_ge(s_accf[bank(prev, 1)], acc_uses(l, prev) + 1 - (N_Q // 2 if phase == 0 else 0))
                src = a["post_g"][ds(l * 4 + phase, 1), :]
                sp.dma_start(post_gain[:, :], src.to_broadcast([P, D])).then_inc(s_gain, 16)

            sp.dma_start(ident[:, :], a["ident"]).then_inc(s_first, 16)
            sp.dma_start(gains[:, :], a["gains"]).then_inc(s_first, 16)
            sp.dma_start(x[:, 0, :], a["x"][0:P, :]).then_inc(s_x_in[0], 16)
            load(0, 0)
            sp.dma_start(x[:, 1, :], a["x"][P:2 * P, :]).then_inc(s_x_in[1], 16)
            load(0, 1)
            for dst, name in ((decay[:, :, :, :].rearrange("p e r i -> p (e r i)"), "decay"),
                              (lv_words[:, :], "lv_mask"),
                              (w_a2[:, :, :].rearrange("r l n -> r (l n)"), "w_a2"), (b_a2[:, :], "b_a2"),
                              (w_ga[:, :, :, :].rearrange("p l k n -> p (l k n)"), "w_ga"),
                              (pos_i[:, :], "positions"), (inv_f[:, :], "inv_freq")):
                sp.dma_start(dst, a[name]).then_inc(s_const, 16)

            def ffn_loads(l, f):
                c0 = C_FFN[f]
                with sp.Fori(0, (FU - 3) // 2) as i:
                    for p in range(2):
                        load(l, c0 + 2 + p, j=i * 2 + 2 + p, extra=i * 4)
                load(l, c0 + FU - 1)
                for ci in range(c0 + FU, c0 + FU + 6):
                    if ci == c0 + FU + 1:
                        load_post_gain(l, (0, 3)[f])
                    load(l, ci)

            with sp.Fori(0, LAYERS) as l:
                ffn_loads(l, 0)
                for ci in range(C_IN, C_FFN2 + 2):
                    if ci == C_IN + 4:
                        load_post_gain(l, 1)
                    if ci == C_KV:
                        sp.wait_ge(s_of, l * 4 + 4)
                        sp.dma_start(mem_t[:, :, :], a["mem"].rearrange("(t p) d -> p t d", p=P)).then_inc(s_mem, 16)
                    if ci == C_KV + 3:
                        load_post_gain(l, 2)
                    load(l, ci)
                ffn_loads(l, 1)
                load(l, N_CH)
                load(l, N_CH + 1)
            for t in range(TT):
                sp.wait_ge(s_x, 4 + 16 * (LAYERS - 1) + 12 + 2 * t + 2)
                sp.dma_start(out[t * P:(t + 1) * P, :], x[:, t, :]).then_inc(s_out, 16)
            for s in range(4):
                sp.wait_ge(s_raw[s], 16 * (LAYERS * HALVES // 4 + 1))
            sp.wait_ge(s_out, 16 * TT)

        @block.tensor
        def _(pe):
            def wait_acc(l, q, t, extra=0):
                pe.wait_ge(s_accf[bank(q, t)], acc_uses(l, q) + extra)

            def wait_split(use, l):
                pe.wait_ge(s_tev, t_no(l, use) + 1)

            def three(o, st_hi, st_lo, mv_hi, mv_lo, first, last):
                pe.matmul(o, st_hi, mv_hi, start=first, stop=False)
                pe.matmul(o, st_hi, mv_lo, start=False, stop=False)
                return pe.matmul(o, st_lo, mv_hi, start=False, stop=last)

            def token_pass(l, ci, q, t, src_hi, src_lo, k_src=0, first=True, last=True, x_ci=0, x_q=0):
                nk = CHUNKS[ci % N_CH][3]
                if first:
                    wait_acc(l, q, t, x_q)
                o = acc[q % 2][t]
                for h in range(2):
                    slot = (2 * ci + h) % 4
                    if t == 0:
                        pe.wait_ge(s_lo, half_no(l, ci, h) + x_ci + 1)
                    for k in range(nk):
                        ks = k_src + h * nk + k
                        sl = slice(t * P, t * P + P)
                        mm = three(o[:, :], src_hi[:, ks, sl], src_lo[:, ks, sl], w_hi[:, slot, k, :],
                                   w_lo[:, slot, k, :], first and h == 0 and k == 0, last and h == 1 and k == nk - 1)
                        if t == 1 and k == nk - 1 and h == 0:
                            mm.then_inc(s_half, 1)
                return mm

            def chunk_pass(l, ci, q, t, src_hi, src_lo, **kw):
                token_pass(l, ci, q, t, src_hi, src_lo, **kw).then_inc(s_acc, 1)

            def column_pass(l, ci, q, t, src_hi, src_lo):
                wait_acc(l, q, t)
                for mt in range(2):
                    c = (2 * t + mt) * P
                    for h in range(2):
                        slot = (2 * ci + h) % 4
                        if t == 0 and mt == 0:
                            pe.wait_ge(s_lo, half_no(l, ci, h) + 1)
                        for k in range(4):
                            mm = three(acc[q % 2][t][:, mt * 256:mt * 256 + 256], w_hi[:, slot, k, c:c + P],
                                       w_lo[:, slot, k, c:c + P], src_hi[:, 4 * h + k, :], src_lo[:, 4 * h + k, :],
                                       h == 0 and k == 0, h == 1 and k == 3)
                        if t == 1 and mt == 1 and h == 0:
                            mm.then_inc(s_half, 1)
                mm.then_inc(s_acc, 1)

            def transposes(l, use, pieces, extra=0):
                n = t_no(l, use)
                if use[:3] != ("x", 0, 0):
                    pe.wait_ge(s_tev, n - 1 + extra)
                for (lo, w), src in pieces:
                    rows = src.shape[1]
                    mm = pe.transpose(tb[t_bank(use)][0:rows, lo:lo + w], src, ident[:, :])
                mm.then_inc(s_t, 1)

            def x_transposes(l, phase, t):
                for half in range(2):
                    pe.wait_ge(s_x, l * 16 + 4 * phase + 2 * t + half + 1)
                    transposes(l, ("x", phase, t, half),
                               [((k * P, P), x[:, t, (4 * half + k) * P:(4 * half + k + 1) * P]) for k in range(4)])

            def wait_x(l, phase, t):
                wait_split(("x", phase, t, 1), l)

            def h_transposes(l, f, j, i=0):
                q = Q_FFN[f] + j
                for t in range(TT):
                    pe.wait_ge(s_accf[bank(q, t)], acc_uses(l, q) + 1 + i)
                transposes(l, ("h", f, j), [(((2 * c + t) * P, P), h_tok[:, j % 2, t, c * P:(c + 1) * P])
                                            for c in range(2) for t in range(TT)], extra=i * 2)

            def ffn(l, f):
                c0, q0, phase = C_FFN[f], Q_FFN[f], (0, 3)[f]

                def up(j, i=0):
                    for t in range(TT):
                        if j == 0:
                            wait_x(l, phase, t)
                        chunk_pass(l, c0 + j, q0 + j, t, xT_hi, xT_lo, x_ci=i * 4, x_q=i)
                        if t == 0:
                            if j == 0:
                                x_transposes(l, phase, 1)
                            else:
                                h_transposes(l, f, j - 1, i)
                up(0)
                with pe.Fori(0, (FU - 3) // 2) as i:
                    for p in range(2):
                        up(1 + p, i)
                up(FU - 2)
                up(FU - 1)
                for d, (n, k0, nk) in enumerate(DOWN):
                    for t in range(TT):
                        if n == 0 and k0 == 0 and t == 0:
                            wait_split(("h", f, FU - 2), l)
                        if n == 0 and k0 + 2 * nk == KF:
                            wait_split(("h", f, FU - 1), l)
                        chunk_pass(l, c0 + FU + d, q0 + FU + n, t, hT_hi, hT_lo, k_src=k0, first=k0 == 0,
                                   last=k0 + 2 * nk == KF)
                        if d == 0 and t == 0:
                            h_transposes(l, f, FU - 1)

            def wait_m(l, use, e):
                pe.wait_ge(s_mf[e], m_no(l, use))

            def level(l, n):
                b = LEVELS[n]
                pe.wait_ge(s_av, l * 8 + n + 1)
                A = av[n % 2].rearrange("p (r i) -> p r i", r=2)
                for e in range(2):
                    wait_m(l, f"lv{n}", e)
                    rows = slice(64 * e, 64 * e + 64)
                    if b == P:
                        for r in range(2):
                            mm = pe.matmul(mb[e][:, r * P:(r + 1) * P], A[rows, r, 0:P], A[rows, r, P:2 * P],
                                           start=True, stop=True)
                    else:
                        for t in range(TT):
                            for r in range(2):
                                tile = A[rows, r, t * P:(t + 1) * P]
                                later = tile.rearrange("p (g two b) -> p g two b", two=2, b=b)[:, :, 1, :]
                                c = (2 * t + r) * 64
                                mm = pe.matmul(mb[e][:, c:c + 64], tile, later, start=True, stop=True)
                    mm.then_inc(s_m[e], 1)

            def mixer(l):
                def after(k):
                    if k == 1:
                        pe.wait_ge(s_gal, l + 1)
                        wait_m(l, "z", 0)
                        for t in range(TT):
                            for kt in range(KD):
                                sl = slice(t * P, t * P + P)
                                mm = three(mb[0][:, t * RANK:(t + 1) * RANK], xT_hi[:, kt, sl], xT_lo[:, kt, sl],
                                           w_ga_hi[:, kt, :], w_ga_lo[:, kt, :], kt == 0, kt == KD - 1)
                        mm.then_inc(s_m[0], 1)
                    if k == 2:
                        pe.wait_ge(s_mf[0], m_no(l, "z") + 1)
                        for t in range(TT):
                            transposes(l, ("ga", t), [((0, P), ga_tok[:, t, :])])
                    if k == 3:
                        wait_split(("ga", 1), l)
                        pe.wait_ge(s_a2, l + 1)
                        wait_m(l, "z", 1)
                        for r in range(2):
                            mm = pe.matmul(mb[1][:, r * TOK:(r + 1) * TOK], w_a2_l[:, r * P:(r + 1) * P], gaT[:, :],
                                           start=True, stop=True)
                        mm.then_inc(s_m[1], 1)
                        for t in range(TT):
                            pe.wait_ge(s_accf[bank(Q_IN, t)], acc_uses(l, Q_IN) + 1)
                            transposes(l, ("gqk", t), [((g * P, P), gqk[:, t, g * P:(g + 1) * P]) for g in range(4)])
                    if k == 4:
                        wait_split(("gqk", 1), l)
                        for e in range(2):
                            wait_m(l, "diag", e)
                            rows = slice(64 * e, 64 * e + 64)
                            for t in range(TT):
                                for r in range(2):
                                    c = (2 * t + r) * P
                                    mm = pe.matmul(mb[e][:, c:c + P], gT[rows, 2 + r, t * P:(t + 1) * P],
                                                   gT[rows, r, t * P:(t + 1) * P], start=True, stop=True)
                            mm.then_inc(s_m[e], 1)
                    if k == 5:
                        level(l, 0)
                        for t in range(TT):
                            pe.wait_ge(s_rope, l * 2 + t + 1)
                            transposes(l, ("rqk", t), [((g * P, P), rqk[:, t, g * P:(g + 1) * P]) for g in range(4)])
                    if k == 6:
                        level(l, 1)
                        wait_split(("rqk", 1), l)
                        for e in range(2):
                            wait_m(l, "rj0", e)
                            rows = slice(64 * e, 64 * e + 64)
                            for r in range(2):
                                mm = pe.matmul(mb[e][:, r * TOK:(r + 1) * TOK], rT[rows, 2 + r, 0:P], rT[rows, r, :],
                                               start=True, stop=True)
                            mm.then_inc(s_m[e], 1)
                    if k == 7:
                        level(l, 2)
                        for e in range(2):
                            wait_m(l, "rj1", e)
                            rows = slice(64 * e, 64 * e + 64)
                            for r in range(2):
                                mm = pe.matmul(mb[e][:, r * P:(r + 1) * P], rT[rows, 2 + r, P:2 * P],
                                               rT[rows, r, P:2 * P], start=True, stop=True)
                            mm.then_inc(s_m[e], 1)
                    if k == 8:
                        level(l, 3)
                        level(l, 4)
                        for t in range(TT):
                            pe.wait_ge(s_accf[bank(Q_IN + 3, t)], acc_uses(l, Q_IN + 3) + 1)
                        for t in range(TT):
                            wait_m(l, "ro", t)
                            for hd in range(HEADS):
                                r, e = hd // 2, hd % 2
                                o = mb[t][:, hd * DV:(hd + 1) * DV]
                                v0 = v_tok[:, 0, hd * DV:(hd + 1) * DV]
                                mm = pe.matmul(o, pr0[:, e, r, t * P:(t + 1) * P], v0, start=True, stop=t == 0)
                                if t == 1:
                                    mm = pe.matmul(o, pr1[:, e, r, :], v_tok[:, 1, hd * DV:(hd + 1) * DV],
                                                   start=False, stop=True)
                            mm.then_inc(s_m[t], 1)
                    if k == 9:
                        level(l, 5)
                        level(l, 6)
                    if k == 10:
                        level(l, 7)
                        for t in range(TT):
                            pe.wait_ge(s_accf[bank(Q_IN + 2, t)], acc_uses(l, Q_IN + 2) + 1)
                        for t in range(TT):
                            wait_m(l, "go", 0)
                            wait_m(l, "go", 1)
                            for hd in range(HEADS):
                                r, e = hd // 2, hd % 2
                                o = mb[t][:, hd * DV:(hd + 1) * DV]
                                c = COL + hd * DV
                                if t == 0:
                                    mm = pe.matmul(o, pg[:, e, r, :], v_tok[:, 0, c:c + DV], start=True, stop=True)
                                else:
                                    pe.matmul(o, pgx[:, e, r, :], v_tok[:, 0, c:c + DV], start=True, stop=False)
                                    mm = pe.matmul(o, pg[:, e, 2 + r, :], v_tok[:, 1, c:c + DV], start=False, stop=True)
                            mm.then_inc(s_m[t], 1)

                x_transposes(l, 1, 0)
                for k in range(12):
                    c, t = k // 2, k % 2
                    if c == 0:
                        wait_x(l, 1, t)
                    chunk_pass(l, C_IN + c, Q_IN + c, t, xT_hi, xT_lo)
                    if k == 0:
                        x_transposes(l, 1, 1)
                    after(k)

            def mixed_transposes(l, t):
                for g in range(2):
                    pe.wait_ge(s_mixed, l * 4 + 2 * g + t + 1)
                    transposes(l, ("mix", t, g), [((k * P, P), o_sb[:, t, (4 * g + k) * P:(4 * g + k + 1) * P])
                                                  for k in range(4)])

            def mem_transposes(l, t):
                pe.wait_ge(s_memn, l * 2 + t + 1)
                for g in range(2):
                    transposes(l, ("mem", t, g), [((k * P, P), mem_t[:, t, (4 * g + k) * P:(4 * g + k + 1) * P])
                                                  for k in range(4)])

            def scores(l, h):
                bk = h % 2
                use = "s0" if h < 2 else "s1"
                wait_m(l, use, bk)
                for t in range(TT):
                    for kk in range(2):
                        mm = pe.matmul(mb[bk][:, t * TOK:(t + 1) * TOK], qT[:, 2 * h + kk, t * P:(t + 1) * P],
                                       kT[:, 2 * h + kk, :], start=kk == 0, stop=kk == 1)
                mm.then_inc(s_m[bk], 1)

            def prob_transposes(l, h):
                pe.wait_ge(s_p, l * XH + h + 1)
                transposes(l, ("p", h), [(((2 * m + t) * P, P), pr[:, h % 2, t, m * P:(m + 1) * P])
                                         for m in range(2) for t in range(TT)])

            def attend(l, h):
                q, t = Q_AV + h // 2, h % 2
                wait_acc(l, q, t)
                wait_split(("p", h), l)
                for dv in range(2):
                    c = h * 256 + dv * P
                    for m in range(2):
                        mm = pe.matmul(acc[q % 2][t][:, dv * TOK:(dv + 1) * TOK], vx[:, m, c:c + P],
                                       pT[:, h % 2, m, :], start=m == 0, stop=m == 1)
                mm.then_inc(s_acc, 1)

            pe.wait_ge(s_first, 32)
            x_transposes(0, 0, 0)
            with pe.Fori(0, LAYERS) as l:
                ffn(l, 0)
                mixer(l)
                mixed_transposes(l, 0)
                wait_split(("mix", 0, 1), l)
                chunk_pass(l, C_OUT, Q_OUT, 0, xT_hi, xT_lo)
                mixed_transposes(l, 1)
                wait_split(("mix", 1, 1), l)
                chunk_pass(l, C_OUT, Q_OUT, 1, xT_hi, xT_lo)
                mem_transposes(l, 0)
                chunk_pass(l, C_OUT + 1, Q_OUT + 1, 0, xT_hi, xT_lo)
                mem_transposes(l, 1)
                chunk_pass(l, C_OUT + 1, Q_OUT + 1, 1, xT_hi, xT_lo)
                wait_split(("mem", 1, 1), l)
                for t in range(TT):
                    column_pass(l, C_KV, Q_KV, t, mT_hi, mT_lo)
                    x_transposes(l, 2, t)
                for t in range(TT):
                    column_pass(l, C_KV + 1, Q_KV + 1, t, mT_hi, mT_lo)
                for c in (2, 3):
                    for t in range(TT):
                        chunk_pass(l, C_KV + c, Q_KV + c, t, mT_hi, mT_lo)
                wait_x(l, 2, 1)
                column_pass(l, C_Q, Q_Q, 0, xT_hi, xT_lo)
                column_pass(l, C_Q, Q_Q, 1, xT_hi, xT_lo)
                column_pass(l, C_Q + 1, Q_Q + 1, 0, xT_hi, xT_lo)
                for t in range(TT):
                    for q in (Q_KV, Q_KV + 1, Q_KV + 2, Q_KV + 3, Q_Q):
                        pe.wait_ge(s_accf[bank(q, t)], acc_uses(l, q) + 1)
                scores(l, 0)
                scores(l, 1)
                column_pass(l, C_Q + 1, Q_Q + 1, 1, xT_hi, xT_lo)
                prob_transposes(l, 0)
                attend(l, 0)
                pe.wait_ge(s_accf[bank(Q_Q + 1, 0)], acc_uses(l, Q_Q + 1) + 1)
                scores(l, 2)
                prob_transposes(l, 1)
                attend(l, 1)
                pe.wait_ge(s_accf[bank(Q_Q + 1, 1)], acc_uses(l, Q_Q + 1) + 1)
                scores(l, 3)
                for h in (2, 3):
                    prob_transposes(l, h)
                    attend(l, h)
                for h in range(XH):
                    q = Q_AV + h // 2
                    pe.wait_ge(s_accf[bank(q, h % 2)], acc_uses(l, q) + 1)
                for c in range(2):
                    for t in range(TT):
                        chunk_pass(l, C_O + c, Q_O + c, t, xT_hi, xT_lo)
                x_transposes(l, 3, 0)
                ffn(l, 1)
                x_transposes(l, 4, 0)

        @block.scalar
        def _(act):
            def split_hi(l, ci, h, i=None):
                lay = l
                if ci >= N_CH:
                    lay = other(l)
                _, _, _, nk, gain = CHUNKS[ci % N_CH]
                slot = (2 * ci + h) % 4
                x4 = 0 if i is None else i * 4
                x1 = 0 if i is None else i
                act.wait_ge(s_raw[slot], (l * (HALVES // 4) + x1 + (2 * ci + h) // 4 + 1) * 16)
                if h == 0:
                    act.wait_ge(s_half, l * N_CH + ci - 1 + x1 * 2)
                elif ci == 1:
                    act.wait_ge(s_acc, l * PASSES)
                else:
                    act.wait_ge(s_acc, chunk_pass_no(l, ci - 2, 1) + 1 + x4)
                if gain is None:
                    act.activation(w_hi[:, slot, 0:nk, :], raw[:, slot, 0:nk, :], ACT.Copy).then_inc(s_hi, 1)
                    return
                act.nop(nofuse=True)
                for k in range(nk):
                    g = lay * (N_GAINS * KD) + gain * KD + h * nk + k
                    ins = act.activation(w_hi[:, slot, k, :], raw[:, slot, k, :], ACT.Copy, scale=gains[:, ds(g, 1)])
                ins.then_inc(s_hi, 1)

            def wait_pass(l, q, t, i=0):
                act.wait_ge(s_acc, pass_no(l, q, t) + 1 + i * 4)

            def t_hi(l, use, dst, cols=COL, extra=0):
                act.wait_ge(s_t, t_no(l, use) + 1 + extra)
                act.activation(dst, tb[t_bank(use)][:, 0:cols], ACT.Copy).then_inc(s_thi, 1)

            def x_hi(l, phase, t):
                for g in range(2):
                    t_hi(l, ("x", phase, t, g), xT_hi[:, 4 * g:4 * g + 4, t * P:(t + 1) * P])

            def x_square(l, phase, t):
                for half in range(2):
                    act.wait_ge(s_x, l * 16 + 4 * phase + 2 * t + half + 1)
                if not (phase == 0 and t == 0):
                    act.wait_ge(s_xsq, l * 8 + 2 * phase + t)
                act.activation(junk_x[:, :], x[:, t, :], ACT.Square, accum_out=xss[:, t:t + 1]).then_inc(s_xsq, 1)

            def y_square(l, phase, q, n, t):
                wait_pass(l, q, t)
                no = l * 16 + 4 * phase + 2 * n + t
                act.wait_ge(s_ysq, no)
                act.activation(junk_y[:, :], acc[q % 2][t][:, :], ACT.Square,
                               accum_out=yss[:, t, n:n + 1]).then_inc(s_ysq, 1)

            def boundary(l, phase, q, ci, hi0, cut=False):
                y_square(l, phase, q, 1, 0)
                split_hi(l, ci + 1, 1)
                x_square(l, phase + 1, 0)
                if hi0:
                    x_hi(l, phase + 1, 0)
                y_square(l, phase, q, 1, 1)

            def ffn(l, f):
                c0, q0, phase = C_FFN[f], Q_FFN[f], (0, 3)[f]
                split_hi(l, c0 + 1, 0)
                x_hi(l, phase, 1)
                x_square(l, phase, 1)

                def h_hi(j, i):
                    if i is None:
                        dst = hT_hi[:, 2 * j:2 * j + 2, :]
                    else:
                        dst = hT_hi[:, ds(i * 4 + 2 * j, 2), :]
                    t_hi(l, ("h", f, j), dst, extra=0 if i is None else i * 2)

                def tanh(j, t, i):
                    x1 = 0 if i is None else i
                    wait_pass(l, q0 + j, t, x1)
                    if j == 0:
                        act.wait_ge(s_rpre, l * 8 + 2 * phase + t + 1)
                    else:
                        act.wait_ge(s_gated, l * 4 * FU + f * 2 * FU + 2 * j + t - 1 + x1 * 4)
                    act.activation(th[:, t, :], acc[(q0 + j) % 2][t][:, 0:256], ACT.Tanh,
                                   scale=r_half[:, t:t + 1]).then_inc(s_tanh, 1)

                def up(j, i=None):
                    tanh(j, 0, i)
                    if j > 0:
                        h_hi(j - 1, i)
                    split_hi(l, c0 + j + 1, 1, i)
                    tanh(j, 1, i)
                    split_hi(l, c0 + j + 2, 0, i)
                up(0)
                with act.Fori(0, (FU - 3) // 2) as i:
                    for p in range(2):
                        up(1 + p, i)
                up(FU - 2)
                up(FU - 1)
                for d in range(6):
                    ci = c0 + FU + d
                    if d == 0:
                        h_hi(FU - 1, None)
                    if d == 3:
                        y_square(l, phase, q0 + FU, 0, 0)
                        y_square(l, phase, q0 + FU, 0, 1)
                    if d < 5:
                        split_hi(l, ci + 1, 1)
                        split_hi(l, ci + 2, 0)
                boundary(l, phase, q0 + FU + 1, c0 + FU + 5, True)

            def exp_decay(l, n):
                act.wait_ge(s_tmp, l * 8 + n + 1)
                act.activation(dec[n % 2], dec[n % 2], ACT.Exp, scale=1.0 / TAU).then_inc(s_dec, 1)

            def head_outputs(l, use, g):
                for t in range(TT):
                    act.wait_ge(s_m[t], m_no(l, use) + 1)
                    if g == 1:
                        act.wait_ge(s_hss, l * 4 + t + 1)
                    sq = (rot_a, rot_b)[t]
                    act.activation(sq[:, :], mb[t][:, :], ACT.Square)
                    act.activation(o_sb[:, t, g * COL:(g + 1) * COL], mb[t][:, :], ACT.Copy).then_inc(s_mf[t], 1)

            def mixer(l):
                def project(c, t, dst, scale):
                    wait_pass(l, Q_IN + c, t)
                    act.activation(dst, acc[(Q_IN + c) % 2][t][:, :], ACT.Copy,
                                   scale=scale[:, t:t + 1]).then_inc(s_accf[bank(Q_IN + c, t)], 1)

                def gate_tanh(c, t):
                    wait_pass(l, Q_IN + c, t)
                    g = c - 4
                    act.activation(gate[:, t, g * COL:(g + 1) * COL], acc[(Q_IN + c) % 2][t][:, :], ACT.Tanh,
                                   scale=r_half[:, t:t + 1]).then_inc(s_gtanh, 1)

                def split_after(k):
                    ci = C_IN + k // 2
                    if k % 2 == 0:
                        split_hi(l, ci + 1, 1)
                    else:
                        split_hi(l, ci + 2, 0)
                act.wait_ge(s_gas, l + 1)
                act.activation(w_ga_hi[:, :, :], w_ga_s[:, :, :], ACT.Copy).then_inc(s_gah, 1)
                split_hi(l, C_IN + 1, 0)
                x_hi(l, 1, 1)
                x_square(l, 1, 1)
                act.wait_ge(s_rpre, l * 8 + 2 + 0 + 1)
                project(0, 0, gqk[:, 0, :], r_pre)
                split_after(0)
                act.wait_ge(s_rpre, l * 8 + 2 + 1 + 1)
                project(0, 1, gqk[:, 1, :], r_pre)
                split_after(1)
                project(1, 0, rqk[:, 0, :], r_pre)
                split_after(2)
                project(1, 1, rqk[:, 1, :], r_pre)
                act.wait_ge(s_mf[1], m_no(l, "z") + 1)
                act.activation(lg, zb, ACT.Abs).then_inc(s_lsig, 1)
                act.wait_ge(s_lsig, l * 3 + 1)
                act.activation(lg, lg, ACT.Exp, scale=-1.0).then_inc(s_lsig, 1)
                act.wait_ge(s_lsig, l * 3 + 2)
                act.activation(lg, lg, ACT.Ln, bias=1.0).then_inc(s_lsig, 1)
                split_after(3)
                project(2, 0, v_tok[:, 0, COL:2 * COL], r_8)
                split_after(4)
                exp_decay(l, 0)
                exp_decay(l, 1)
                project(2, 1, v_tok[:, 1, COL:2 * COL], r_8)
                split_after(5)
                exp_decay(l, 2)
                exp_decay(l, 3)
                project(3, 0, v_tok[:, 0, 0:COL], r_pre)
                split_after(6)
                exp_decay(l, 4)
                project(3, 1, v_tok[:, 1, 0:COL], r_pre)
                split_after(7)
                exp_decay(l, 5)
                gate_tanh(4, 0)
                split_after(8)
                exp_decay(l, 6)
                head_outputs(l, "ro", 0)
                gate_tanh(4, 1)
                split_after(9)
                exp_decay(l, 7)
                gate_tanh(5, 0)
                head_outputs(l, "go", 1)
                split_after(10)

                def mix_hi(t):
                    for g in range(2):
                        t_hi(l, ("mix", t, g), xT_hi[:, 4 * g:4 * g + 4, t * P:(t + 1) * P])
                gate_tanh(5, 1)
                mix_hi(0)
                split_after(11)
                mix_hi(1)

            def mem_hi(l, t):
                for g in range(2):
                    t_hi(l, ("mem", t, g), mT_hi[:, 4 * g:4 * g + 4, t * P:(t + 1) * P])

            def mix_out(l):
                act.wait_ge(s_mem, l * 16 + 16)
                for t in range(TT):
                    if t == 1:
                        act.wait_ge(s_msq, l * 2 + 1)
                    else:
                        act.wait_ge(s_xsq, l * 8 + 4)
                    act.activation(junk_x[:, :], mem_t[:, t, :], ACT.Square,
                                   accum_out=mss[:, t:t + 1]).then_inc(s_msq, 1)
                y_square(l, 1, Q_OUT, 0, 0)
                split_hi(l, C_OUT + 1, 1)
                y_square(l, 1, Q_OUT, 0, 1)
                mem_hi(l, 0)
                split_hi(l, C_OUT + 2, 0)
                y_square(l, 1, Q_OUT + 1, 1, 0)
                mem_hi(l, 1)
                split_hi(l, C_OUT + 2, 1)
                act.wait_ge(s_msq, l * 2 + 2)
                x_square(l, 2, 0)
                y_square(l, 1, Q_OUT + 1, 1, 1)
                split_hi(l, C_KV + 1, 0)

            def attention(l):
                def copy_out(q, t, dst):
                    wait_pass(l, q, t)
                    act.activation(dst, acc[q % 2][t][:, :], ACT.Copy).then_inc(s_accf[bank(q, t)], 1)
                x_hi(l, 2, 0)
                copy_out(Q_KV, 0, kT[:, 0:2, :])
                split_hi(l, C_KV + 1, 1)
                x_hi(l, 2, 1)
                copy_out(Q_KV, 1, kT[:, 2:4, :])
                x_square(l, 2, 1)
                split_hi(l, C_KV + 2, 0)
                for c in (1, 2, 3):
                    for t in range(TT):
                        dst = kT[:, 4 + 2 * t:6 + 2 * t, :] if c == 1 else vx[:, t, (c - 2) * COL:(c - 1) * COL]
                        copy_out(Q_KV + c, t, dst)
                        split_hi(l, C_KV + c + 1 + t, 1 - t)
                split_hi(l, C_Q + 1, 1)
                split_hi(l, C_Q + 2, 0)

                def exp_scores(h):
                    act.wait_ge(s_nb, l * XH + h + 1)
                    for t in range(TT):
                        ins = act.activation(pr[:, h % 2, t, :], mb[h % 2][:, t * TOK:(t + 1) * TOK], ACT.Exp,
                                             bias=nbias[:, h, t:t + 1], scale=r_16[:, t:t + 1],
                                             accum_out=rsum[:, h, t:t + 1])
                    ins.then_inc(s_mf[h % 2], 1)

                def head_hi(h):
                    q = Q_AV + h // 2
                    wait_pass(l, q, h % 2)
                    act.activation(xT_hi[:, 2 * h:2 * h + 2, :], acc[q % 2][h % 2][:, :], ACT.Copy).then_inc(s_ohi, 1)
                exp_scores(0)
                exp_scores(1)
                split_hi(l, C_O, 1)
                head_hi(0)
                exp_scores(2)
                head_hi(1)
                exp_scores(3)
                split_hi(l, C_O + 1, 0)
                head_hi(2)
                head_hi(3)
                y_square(l, 2, Q_O, 0, 0)
                split_hi(l, C_O + 1, 1)
                y_square(l, 2, Q_O, 0, 1)
                split_hi(l, C_O + 2, 0)
                boundary(l, 2, Q_O + 1, C_O + 1, True)

            act.wait_ge(s_first, 32)
            for h in range(2):
                act.wait_ge(s_raw[h], 16)
                for k in range(4):
                    ins = act.activation(w_hi[:, h, k, :], raw[:, h, k, :], ACT.Copy,
                                         scale=gains[:, G_FFN1 * KD + 4 * h + k:G_FFN1 * KD + 4 * h + k + 1])
                ins.then_inc(s_hi, 1)
            x_hi(0, 0, 0)
            x_square(0, 0, 0)
            act.wait_ge(s_setup, 11)
            act.activation(sin_t[:, :, :], rest[3][:, :, :], ACT.Sin).then_inc(s_trig, 1)
            act.activation(cos_t[:, :, :], carg[:, :, :], ACT.Sin).then_inc(s_trig, 1)
            with act.Fori(0, LAYERS) as l:
                ffn(l, 0)
                mixer(l)
                mix_out(l)
                attention(l)
                ffn(l, 1)

        @block.vector
        def _(dve):
            def split_lo(l, ci, h, i=None):
                lay = l
                if ci >= N_CH:
                    lay = other(l)
                _, _, _, nk, gain = CHUNKS[ci % N_CH]
                slot = (2 * ci + h) % 4
                dve.wait_ge(s_hi, half_no(l, ci, h) + (0 if i is None else i * 4) + 1)
                if gain is None:
                    dve.tensor_tensor(w_lo[:, slot, 0:nk, :], raw[:, slot, 0:nk, :],
                                      w_hi[:, slot, 0:nk, :].bitcast(F32), ALU.subtract).then_inc(s_lo, 1)
                    return
                for k in range(nk):
                    g = lay * (N_GAINS * KD) + gain * KD + h * nk + k
                    ins = dve.scalar_tensor_tensor(w_lo[:, slot, k, :], raw[:, slot, k, :], gains[:, ds(g, 1)],
                                                   w_hi[:, slot, k, :].bitcast(F32), ALU.mult, ALU.subtract)
                ins.then_inc(s_lo, 1)

            def t_lo(l, use, dst, hi, extra_t=0, extra_s=0):
                dve.wait_ge(s_thi, ts_no(l, use) + 1 + extra_s)
                dve.tensor_tensor(dst, tb[t_bank(use)][:, :].rearrange("p (k n) -> p k n", k=dst.shape[1]),
                                  hi.bitcast(F32), ALU.subtract).then_inc(s_tev, 1)

            def t_copy(l, use, dst, rows=P, cols=COL):
                dve.wait_ge(s_t, t_no(l, use) + 1)
                src = tb[t_bank(use)][0:rows, 0:cols]
                if len(dst.shape) == 3:
                    src = src.rearrange("p (k n) -> p k n", k=dst.shape[1])
                dve.tensor_copy(dst, src).then_inc(s_tev, 1)

            def x_lo(l, phase, t):
                for g in range(2):
                    s = (slice(None), slice(4 * g, 4 * g + 4), slice(t * P, (t + 1) * P))
                    t_lo(l, ("x", phase, t, g), xT_lo[s], xT_hi[s])

            def y_gain(l, phase, q, n, t):
                if n == 0 and t == 0:
                    dve.wait_ge(s_gain, (l * 4 + phase + 1) * 16)
                dve.wait_ge(s_ysq, l * 16 + 4 * phase + 2 * n + t + 1)
                dve.tensor_tensor(yg[:, t, n * COL:(n + 1) * COL], acc[q % 2][t][:, :],
                                  post_gain[:, n * COL:(n + 1) * COL], ALU.mult).then_inc(s_accf[bank(q, t)], 1)

            def x_update(l, phase, q, t):
                dve.wait_ge(s_rpost, l * 8 + 2 * phase + t + 1)
                dve.wait_ge(s_accf[bank(q, t)], acc_uses(l, q) + 1)
                for n in range(2):
                    s = slice(n * COL, (n + 1) * COL)
                    dve.scalar_tensor_tensor(x[:, t, s], yg[:, t, s], r_post[:, t:t + 1], x[:, t, s],
                                             ALU.mult, ALU.add).then_inc(s_x, 1)

            def boundary(l, phase, q, ci, lo0):
                y_gain(l, phase, q, 1, 0)
                x_update(l, phase, q, 0)
                split_lo(l, ci + 1, 1)
                if lo0:
                    x_lo(l, phase + 1, 0)
                y_gain(l, phase, q, 1, 1)
                x_update(l, phase, q, 1)

            def ffn(l, f):
                c0, q0, phase = C_FFN[f], Q_FFN[f], (0, 3)[f]
                split_lo(l, c0 + 1, 0)
                x_lo(l, phase, 1)

                def h_lo(j, i):
                    if i is None:
                        s = (slice(None), slice(2 * j, 2 * j + 2), slice(None))
                    else:
                        s = (slice(None), ds(i * 4 + 2 * j, 2), slice(None))
                    t_lo(l, ("h", f, j), hT_lo[s], hT_hi[s], extra_s=0 if i is None else i * 2)

                def gated(j, t, i):
                    base = l * 4 * FU + f * 2 * FU + 2 * j + t + 1 + (0 if i is None else i * 4)
                    b = acc[(q0 + j) % 2][t]
                    dve.wait_ge(s_tanh, base)
                    dve.scalar_tensor_tensor(gt[:, t, :], th[:, t, :], 1.0, b[:, 0:256], ALU.add,
                                             ALU.mult).then_inc(s_gated, 1)
                    dve.wait_ge(s_gated, base)
                    dve.scalar_tensor_tensor(h_tok[:, j % 2, t, :], gt[:, t, :], c_half[:, t:t + 1], b[:, 256:512],
                                             ALU.mult, ALU.mult).then_inc(s_accf[bank(q0 + j, t)], 1)

                def up(j, i=None):
                    gated(j, 0, i)
                    if j > 0:
                        h_lo(j - 1, i)
                    split_lo(l, c0 + j + 1, 1, i)
                    gated(j, 1, i)
                    split_lo(l, c0 + j + 2, 0, i)
                up(0)
                with dve.Fori(0, (FU - 3) // 2) as i:
                    for p in range(2):
                        up(1 + p, i)
                up(FU - 2)
                up(FU - 1)
                for d in range(6):
                    ci = c0 + FU + d
                    if d == 0:
                        h_lo(FU - 1, None)
                    if d == 3:
                        y_gain(l, phase, q0 + FU, 0, 0)
                        y_gain(l, phase, q0 + FU, 0, 1)
                    if d < 5:
                        split_lo(l, ci + 1, 1)
                        split_lo(l, ci + 2, 0)
                boundary(l, phase, q0 + FU + 1, c0 + FU + 5, True)

            def mixer(l):
                def split_after(k):
                    ci = C_IN + k // 2
                    if k % 2 == 0:
                        split_lo(l, ci + 1, 1)
                    else:
                        split_lo(l, ci + 2, 0)

                def level_out(n):
                    b = LEVELS[n]
                    for e in range(2):
                        dve.wait_ge(s_m[e], m_no(l, f"lv{n}") + 1)
                        if b == P:
                            dve.tensor_copy(pgx[:, e].rearrange("p r i -> p (r i)"), mb[e][:, 0:2 * P]).then_inc(s_mf[e], 1)
                            continue
                        dve.wait_ge(s_mf[e], m_no(l, f"lv{n}"))
                        dst = pg[:, e].rearrange("p c (g two b) -> p c g two b", two=2, b=b)[:, :, :, 1, :]
                        src = mb[e][:, 0:4 * 64].rearrange("p (c g b) -> p c g b", c=4, b=b)
                        msk = lv_mask[:, n - 1, :].rearrange("p (g b) -> p g b", b=b)
                        msk = msk.unsqueeze(1).to_broadcast([P, 4, 64 // b, b])
                        dve.nop(nofuse=True)
                        dve.copy_predicated(dst, msk, src).then_inc(s_mf[e], 1)

                def retention_mask(j):
                    for e in range(2):
                        dve.wait_ge(s_m[e], m_no(l, f"rj{j}") + 1)
                        w = TOK if j == 0 else P
                        dst = (pr0, pr1)[j][:, e]
                        dve.tensor_tensor(dst, mb[e][:, 0:2 * w].rearrange("p (r i) -> p r i", r=2),
                                          decay[:, e, :, 0:w], ALU.mult).then_inc(s_mf[e], 1)

                def head_squares(use, g):
                    for t in range(TT):
                        dve.wait_ge(s_mf[t], m_no(l, use) + 1)
                        sq = (rot_a, rot_b)[t]
                        dve.tensor_reduce(hss[:, t, 4 * g:4 * g + 4], sq[:, :].rearrange("p (h d) -> p h d", h=HEADS),
                                          AX.X, ALU.add).then_inc(s_hss, 1)

                def gate_z(c, t):
                    g = c - 4
                    dve.wait_ge(s_gtanh, l * 4 + 2 * g + t + 1)
                    s = gate[:, t, g * COL:(g + 1) * COL]
                    dve.scalar_tensor_tensor(s, s, 1.0, acc[(Q_IN + c) % 2][t][:, :], ALU.add,
                                             ALU.mult).then_inc(s_accf[bank(Q_IN + c, t)], 1)

                def mixed(c, t):
                    g = c - 4
                    q = Q_IN + c
                    dve.wait_ge(s_accf[bank(q, t)], acc_uses(l, q) + 1)
                    dve.wait_ge(s_of, l * 4 + 2 * g + t + 1)
                    s = (slice(None), t, slice(g * COL, (g + 1) * COL))
                    dve.tensor_tensor(o_sb[s], o_sb[s], gate[s], ALU.mult).then_inc(s_mixed, 1)

                g_mix = gains[:, ds(l * (N_GAINS * KD) + G_MIX * KD, KD)].unsqueeze(2).to_broadcast([P, KD, RANK])
                dve.tensor_tensor(w_ga_s[:, :, :], w_ga[:, ds(l, 1), :, :].rearrange("p o k n -> p (o k) n"), g_mix,
                                  ALU.mult).then_inc(s_gas, 1)
                split_lo(l, C_IN + 1, 0)
                x_lo(l, 1, 1)
                dve.wait_ge(s_gah, l + 1)
                dve.tensor_tensor(w_ga_lo[:, :, :], w_ga_s[:, :, :], w_ga_hi[:, :, :].bitcast(F32),
                                  ALU.subtract).then_inc(s_gal, 1)
                split_after(0)
                dve.wait_ge(s_m[0], m_no(l, "z") + 1)
                dve.wait_ge(s_rpre, l * 8 + 2 + 1 + 1)
                for t in range(TT):
                    ins = dve.tensor_scalar(ga_tok[:, t, :], mb[0][:, t * RANK:(t + 1) * RANK], r_pre[:, t:t + 1], None,
                                            ALU.mult)
                ins.then_inc(s_mf[0], 1)
                split_after(1)
                for t in range(TT):
                    t_copy(l, ("ga", t), gaT[:, t * P:(t + 1) * P], RANK, P)
                split_after(2)
                dve.wait_ge(s_m[1], m_no(l, "z") + 1)
                dve.tensor_tensor(zb, mb[1][:, :].rearrange("p (r i) -> p r i", r=2),
                                  b_a2[:, ds(l * 2, 2)].unsqueeze(2).to_broadcast([P, 2, TOK]),
                                  ALU.add).then_inc(s_mf[1], 1)
                for t in range(TT):
                    t_copy(l, ("gqk", t), gT[:, :, t * P:(t + 1) * P])
                split_after(3)
                dve.wait_ge(s_lsig, l * 3 + 3)
                dve.scalar_tensor_tensor(zb, zb, 0.0, lg, ALU.min, ALU.subtract).then_inc(s_la, 1)
                dve.wait_ge(s_la, l + 1)
                for r in range(2):
                    for t in range(TT):
                        dve.tensor_tensor_scan(cum[:, r, t * P:(t + 1) * P], ones[:, :], zb[:, r, t * P:(t + 1) * P], 0.0,
                                               ALU.mult, ALU.add).then_inc(s_cum, 1)
                for e in range(2):
                    dve.wait_ge(s_m[e], m_no(l, "diag") + 1)
                    dve.tensor_tensor(pg[:, e], mb[e][:, :].rearrange("p (c i) -> p c i", c=4),
                                      ident[:, :].unsqueeze(1).to_broadcast([P, 4, P]), ALU.mult).then_inc(s_mf[e], 1)
                split_after(4)
                level_out(0)
                for t in range(TT):
                    t_copy(l, ("rqk", t), rT[:, :, t * P:(t + 1) * P])
                split_after(5)
                level_out(1)
                retention_mask(0)
                split_after(6)
                level_out(2)
                retention_mask(1)
                split_after(7)
                gate_z(4, 0)
                level_out(3)
                level_out(4)
                head_squares("ro", 0)
                split_after(8)
                gate_z(4, 1)
                level_out(5)
                level_out(6)
                split_after(9)
                for t in range(TT):
                    mixed(4, t)
                gate_z(5, 0)
                level_out(7)
                head_squares("go", 1)
                split_after(10)
                mixed(5, 0)

                def mix_lo(t):
                    for g in range(2):
                        s = (slice(None), slice(4 * g, 4 * g + 4), slice(t * P, (t + 1) * P))
                        t_lo(l, ("mix", t, g), xT_lo[s], xT_hi[s])
                gate_z(5, 1)
                mix_lo(0)
                mixed(5, 1)
                split_after(11)
                mix_lo(1)

            def mem_lo(l, t):
                for g in range(2):
                    s = (slice(None), slice(4 * g, 4 * g + 4), slice(t * P, (t + 1) * P))
                    t_lo(l, ("mem", t, g), mT_lo[s], mT_hi[s])

            def mix_out(l):
                y_gain(l, 1, Q_OUT, 0, 0)
                for t in range(TT):
                    dve.wait_ge(s_rmem, l * 2 + t + 1)
                    dve.tensor_scalar(mem_t[:, t, :], mem_t[:, t, :], r_mem[:, t:t + 1], None,
                                      ALU.mult).then_inc(s_memn, 1)
                split_lo(l, C_OUT + 1, 1)
                y_gain(l, 1, Q_OUT, 0, 1)
                mem_lo(l, 0)
                split_lo(l, C_OUT + 2, 0)
                y_gain(l, 1, Q_OUT + 1, 1, 0)
                mem_lo(l, 1)
                x_update(l, 1, Q_OUT + 1, 0)
                split_lo(l, C_OUT + 2, 1)
                y_gain(l, 1, Q_OUT + 1, 1, 1)
                x_update(l, 1, Q_OUT + 1, 1)
                split_lo(l, C_KV + 1, 0)

            def attention(l):
                x_lo(l, 2, 0)
                split_lo(l, C_KV + 1, 1)
                x_lo(l, 2, 1)
                split_lo(l, C_KV + 2, 0)
                for c in (1, 2, 3):
                    for t in range(TT):
                        split_lo(l, C_KV + c + 1 + t, 1 - t)

                def q_copy(c, t):
                    q = Q_Q + c
                    dve.wait_ge(s_acc, pass_no(l, q, t) + 1)
                    dve.tensor_copy(qT[:, 4 * c + 2 * t:4 * c + 2 * t + 2, :].rearrange("p k i -> p (k i)"),
                                    acc[q % 2][t][:, :]).then_inc(s_accf[bank(q, t)], 1)

                def m_use(h):
                    return m_no(l, "s0" if h < 2 else "s1")

                def bias(h):
                    dve.wait_ge(s_m[h % 2], m_use(h) + 1)
                    dve.tensor_reduce(smax[:, h, :], mb[h % 2][:, :].rearrange("p (t m) -> p t m", t=TT), AX.X,
                                      ALU.max).then_inc(s_smax, 1)
                    dve.wait_ge(s_smax, l * XH + h + 1)
                    dve.wait_ge(s_rpre, l * 8 + 2 * 2 + 1 + 1)
                    dve.tensor_tensor(nbias[:, h, :], smax[:, h, :], n_16[:, :], ALU.mult).then_inc(s_nb, 1)

                def normalise(h):
                    dve.wait_ge(s_mf[h % 2], m_use(h) + 1)
                    dve.reciprocal(rinv[:, h, :], rsum[:, h, :]).then_inc(s_rinv, 1)
                    dve.wait_ge(s_rinv, l * XH + h + 1)
                    for t in range(TT):
                        ins = dve.tensor_scalar(pr[:, h % 2, t, :], pr[:, h % 2, t, :], rinv[:, h, t:t + 1], None,
                                                ALU.mult)
                    ins.then_inc(s_p, 1)

                def p_copy(h):
                    t_copy(l, ("p", h), pT[:, h % 2])

                def head_lo(h):
                    q = Q_AV + h // 2
                    dve.wait_ge(s_ohi, l * XH + h + 1)
                    s = (slice(None), slice(2 * h, 2 * h + 2), slice(None))
                    dve.tensor_tensor(xT_lo[s], acc[q % 2][h % 2][:, :].rearrange("p (k i) -> p k i", k=2),
                                      xT_hi[s].bitcast(F32), ALU.subtract).then_inc(s_accf[bank(q, h % 2)], 1)
                q_copy(0, 0)
                split_lo(l, C_Q + 1, 1)
                q_copy(0, 1)
                split_lo(l, C_Q + 2, 0)
                q_copy(1, 0)
                bias(0)
                bias(1)
                normalise(0)
                normalise(1)
                split_lo(l, C_O, 1)
                q_copy(1, 1)
                p_copy(0)
                head_lo(0)
                bias(2)
                p_copy(1)
                normalise(2)
                head_lo(1)
                bias(3)
                normalise(3)
                split_lo(l, C_O + 1, 0)
                p_copy(2)
                head_lo(2)
                p_copy(3)
                head_lo(3)
                y_gain(l, 2, Q_O, 0, 0)
                split_lo(l, C_O + 1, 1)
                y_gain(l, 2, Q_O, 0, 1)
                split_lo(l, C_O + 2, 0)
                boundary(l, 2, Q_O + 1, C_O + 1, True)

            dve.wait_ge(s_x_in[0], 16)
            dve.memset(ones[:, :], 1.0).then_inc(s_x, 2)
            dve.wait_ge(s_first, 32)
            for h in range(2):
                dve.wait_ge(s_hi, h + 1)
                for k in range(4):
                    g = G_FFN1 * KD + 4 * h + k
                    ins = dve.scalar_tensor_tensor(w_lo[:, h, k, :], raw[:, h, k, :], gains[:, g:g + 1],
                                                   w_hi[:, h, k, :].bitcast(F32), ALU.mult, ALU.subtract)
                ins.then_inc(s_lo, 1)
            x_lo(0, 0, 0)
            dve.wait_ge(s_x_in[1], 16)
            dve.memset(ang[:, :, :], 0.0).then_inc(s_x, 2)
            dve.wait_ge(s_const, 16 * 7)
            n_set = [0]

            def setup(ins):
                n_set[0] += 1
                ins.then_inc(s_setup, 1)
                dve.wait_ge(s_setup, n_set[0])

            def flat(t):
                return t[:, :, :].rearrange("p t f -> p (t f)")
            two_pi = 2.0 * np.pi
            c1 = 6.28125
            c2 = float(np.float32(np.round((two_pi - c1) * 2 ** 21) / 2 ** 21))
            c3 = float(two_pi - c1 - c2)
            magic = 1.5 * 2.0 ** 23
            setup(dve.tensor_copy(pos_f[:, :], pos_i[:, :]))
            setup(dve.tensor_tensor(ang[:, :, :], pos_f[:, :].unsqueeze(2).to_broadcast([P, TT, 32]),
                                    inv_f[:, :].unsqueeze(1).to_broadcast([P, TT, 32]), ALU.mult))
            setup(dve.tensor_scalar(flat(turns), flat(ang), 1.0 / two_pi, None, ALU.mult))
            setup(dve.tensor_scalar(flat(turns), flat(turns), magic, None, ALU.add))
            setup(dve.tensor_scalar(flat(turns), flat(turns), -magic, None, ALU.add))
            setup(dve.scalar_tensor_tensor(flat(rest[0]), flat(turns), -c1, flat(ang), ALU.mult, ALU.add))
            setup(dve.scalar_tensor_tensor(flat(rest[1]), flat(turns), -c2, flat(rest[0]), ALU.mult, ALU.add))
            setup(dve.scalar_tensor_tensor(flat(rest[2]), flat(turns), -c3, flat(rest[1]), ALU.mult, ALU.add))
            setup(dve.tensor_scalar(flat(rest[3]), flat(rest[2]), 3.1415925, -3.1415925, ALU.min, ALU.max))
            setup(dve.scalar_tensor_tensor(flat(absr), flat(rest[3]), -1.0, flat(rest[3]), ALU.mult, ALU.max))
            setup(dve.tensor_scalar(flat(carg), flat(absr), -1.0, float(np.pi / 2), ALU.mult, ALU.add))
            dve.wait_ge(s_trig, 2)
            dve.tensor_copy(rope_c[:, :, 0:32], cos_t[:, :, :])
            dve.tensor_copy(rope_c[:, :, 32:64], cos_t[:, :, :])
            dve.tensor_scalar(rope_s[:, :, 0:32], sin_t[:, :, :], -1.0, None, ALU.mult)
            dve.tensor_copy(rope_s[:, :, 32:64], sin_t[:, :, :]).then_inc(s_rope_t, 1)
            with dve.Fori(0, LAYERS) as l:
                ffn(l, 0)
                mixer(l)
                mix_out(l)
                attention(l)
                ffn(l, 1)

        @block.gpsimd
        def _(pool):
            class Steps:

                def __init__(self, start, per_layer):
                    self.start, self.per_layer, self.n, self.l = start, per_layer, 0, 0

                def value(self):
                    return self.start + self.l * self.per_layer + self.n

                def layer(self, l):
                    self.l, self.n = l, 0

            steps = Steps(1, POOL_STEPS)

            def then(ins):
                ins.then_inc(s_pool, 1)
                steps.n += 1
                pool.wait_ge(s_pool, steps.value())

            def post(l, phase, t):
                scale = 4.0 if phase in (0, 3) else 1.0
                pool.wait_ge(s_ysq, l * 16 + 4 * phase + 2 + t + 1)
                c = slice(t, t + 1)
                then(pool.tensor_tensor(v_post[:, c], yss[:, t, 0:1], yss[:, t, 1:2], ALU.add))
                pool.nop(nofuse=True)
                then(pool.tensor_scalar(v_post[:, c], v_post[:, c], scale / D, scale * EPS, ALU.mult, ALU.add))
                pool.tensor_tensor(r_post[:, c], v_post[:, c], half_neg[:, 0:1], ALU.pow).then_inc(s_rpost, 1)

            def pre(l, phase, t):
                pool.wait_ge(s_xsq, l * 8 + 2 * phase + t + 1)
                c = slice(t, t + 1)
                pool.nop(nofuse=True)
                then(pool.tensor_scalar(v_pre[:, c], xss[:, c], 1.0 / D, EPS, ALU.mult, ALU.add))
                then(pool.tensor_tensor(r_pre[:, c], v_pre[:, c], half_neg[:, 0:1], ALU.pow))
                pool.nop(nofuse=True)
                pool.tensor_scalar(r_8[:, c], r_pre[:, c], DK ** -0.5, 0.0, ALU.mult, ALU.add)
                pool.tensor_scalar(r_16[:, c], r_pre[:, c], 1.0 / 16, 0.0, ALU.mult, ALU.add)
                pool.tensor_scalar(n_16[:, c], r_pre[:, c], -1.0 / 16, 0.0, ALU.mult, ALU.add)
                then(pool.tensor_scalar(r_half[:, c], r_pre[:, c], 0.5, 0.0, ALU.mult, ALU.add))
                pool.tensor_tensor(c_half[:, c], r_half[:, c], r_pre[:, c], ALU.mult).then_inc(s_rpre, 1)

            def rope(l, t):
                q = Q_IN + 1
                pool.wait_ge(s_accf[bank(q, t)], acc_uses(l, q) + 1)
                if t == 1:
                    pool.wait_ge(s_rope, l * 2 + 1)
                z = rqk[:, t, :].rearrange("p (h d) -> p h d", h=8)
                ra = rot_a[:, :].rearrange("p (h d) -> p h d", h=8)
                rb = rot_b[:, :].rearrange("p (h d) -> p h d", h=8)
                pool.tensor_tensor(ra, z, rope_c[:, t, :].unsqueeze(1).to_broadcast([P, 8, DK]), ALU.mult)
                for half in range(2):
                    o, i = slice(32 * half, 32 * half + 32), slice(32 - 32 * half, 64 - 32 * half)
                    ins = pool.tensor_tensor(rb[:, :, o], z[:, :, i],
                                             rope_s[:, t, o].unsqueeze(1).to_broadcast([P, 8, 32]), ALU.mult)
                then(ins)
                pool.tensor_tensor(rqk[:, t, :], rot_a[:, :], rot_b[:, :], ALU.add).then_inc(s_rope, 1)

            def blocks(ap, b):
                return ap.rearrange("p (g two b) -> p g two b", two=2, b=b)

            def exponents(l, n):
                b = LEVELS[n]
                if n >= 2:
                    pool.wait_ge(s_av, l * 8 + n - 1)
                e = dec[n % 2]
                if b == P:
                    e3 = e.rearrange("p (r i) -> p r i", r=2)
                    pool.tensor_tensor(e3[:, :, 0:P], cum[:, :, P - 1:P].to_broadcast([P, 2, P]), cum[:, :, 0:P],
                                       ALU.subtract)
                    pool.tensor_copy(e3[:, :, P:2 * P], cum[:, :, P:2 * P]).then_inc(s_tmp, 1)
                    return
                eb, cb = blocks(e, b), blocks(cum[:, :, :].rearrange("p r i -> p (r i)"), b)
                ref = cb[:, :, 0, b - 1:b].to_broadcast([P, 256 // b, b])
                pool.tensor_tensor(eb[:, :, 0, :], ref, cb[:, :, 0, :], ALU.subtract)
                pool.tensor_tensor(eb[:, :, 1, :], cb[:, :, 1, :], ref, ALU.subtract).then_inc(s_tmp, 1)

            def decayed(l, n):
                b = LEVELS[n]
                pool.wait_ge(s_dec, l * 8 + n + 1)
                if n >= 2:
                    pool.wait_ge(s_m[1], m_no(l, f"lv{n - 2}") + 1)
                o, d = blocks(av[n % 2], b), blocks(dec[n % 2], b)
                k = blocks(gT[:, 2:4, :].rearrange("p r i -> p (r i)"), b)
                q = blocks(gT[:, 0:2, :].rearrange("p r i -> p (r i)"), b)
                pool.tensor_tensor(o[:, :, 0, :], k[:, :, 0, :], d[:, :, 0, :], ALU.mult)
                pool.tensor_tensor(o[:, :, 1, :], q[:, :, 1, :], d[:, :, 1, :], ALU.mult).then_inc(s_av, 1)

            def heads(l, g):
                pool.wait_ge(s_hss, l * 4 + 2 * g + 2)
                s = (slice(None), slice(None), slice(4 * g, 4 * g + 4))
                hn = half_neg[:, :].rearrange("p (t h) -> p t h", t=TT)
                pool.nop(nofuse=True)
                then(pool.tensor_scalar(v_head[s], hss[s], 1.0 / DV, EPS, ALU.mult, ALU.add))
                then(pool.tensor_tensor(r_head[s], v_head[s], hn, ALU.pow))
                then(pool.tensor_tensor(f_head[s], r_head[s], r_half[:, :].unsqueeze(2).to_broadcast([P, TT, 4]),
                                        ALU.mult))
                for t in range(TT):
                    o = o_sb[:, t, g * COL:(g + 1) * COL].rearrange("p (h d) -> p h d", h=HEADS)
                    pool.tensor_tensor(o, o, f_head[:, t, 4 * g:4 * g + 4].unsqueeze(2).to_broadcast([P, HEADS, DV]),
                                       ALU.mult).then_inc(s_of, 1)

            def mem_norm(l, t):
                pool.wait_ge(s_msq, l * 2 + t + 1)
                c = slice(t, t + 1)
                pool.nop(nofuse=True)
                then(pool.tensor_scalar(v_mem[:, c], mss[:, c], 1.0 / D, EPS, ALU.mult, ALU.add))
                pool.tensor_tensor(r_mem[:, c], v_mem[:, c], half_neg[:, 0:1], ALU.pow).then_inc(s_rmem, 1)

            def mixer(l):
                pre(l, 1, 1)
                pool.tensor_copy(w_a2_l[:, :], w_a2[:, ds(l, 1), :].rearrange("r o n -> r (o n)")).then_inc(s_a2, 1)
                rope(l, 0)
                rope(l, 1)
                pool.wait_ge(s_cum, l * 4 + 4)
                pool.wait_ge(s_tev, t_no(l, ("gqk", 1)) + 1)
                exponents(l, 0)
                exponents(l, 1)
                for n in range(8):
                    decayed(l, n)
                    if n + 2 < 8:
                        exponents(l, n + 2)
                    if n == 6:
                        heads(l, 0)
                heads(l, 1)

            pool.memset(half_neg[:, :], -0.5).then_inc(s_pool, 1)
            pool.wait_ge(s_pool, 1)
            steps.start = 1
            pre(0, 0, 0)
            steps.start += steps.n
            pool.wait_ge(s_const, 16 * 7)
            pool.wait_ge(s_rope_t, 1)
            with pool.Fori(0, LAYERS) as l:
                steps.layer(l)
                pre(l, 0, 1)
                post(l, 0, 0)
                pre(l, 1, 0)
                post(l, 0, 1)
                mixer(l)
                for t in range(TT):
                    mem_norm(l, t)
                post(l, 1, 0)
                pre(l, 2, 0)
                post(l, 1, 1)
                pre(l, 2, 1)
                post(l, 2, 0)
                pre(l, 3, 0)
                post(l, 2, 1)
                pre(l, 3, 1)
                post(l, 3, 0)
                pre(l, 4, 0)
                post(l, 3, 1)
                assert steps.n == POOL_STEPS, steps.n


def constants():
    gamma_log = np.log1p(-np.exp2(-5.0 - np.arange(HEADS)))
    j, i = np.arange(P)[:, None], np.arange(TOK)[None, :]
    decay = np.zeros((P, 2, 2, TOK))
    for h in range(HEADS):
        decay[:, h % 2, h // 2, :] = np.where(i >= j, np.exp(np.where(i >= j, i - j, 0) * gamma_log[h]), 0.0) * DK ** -0.5
    mask = np.zeros((P, 7, 64), np.int8)
    for v, b in enumerate(LEVELS[1:]):
        for n in range(64):
            first = 2 * b * (n // b)
            mask[first:first + b, v, n] = 1
    inv_freq = 10000.0 ** (-np.arange(0, DK, 2, dtype=np.float64) / DK)
    return {
        "ident": np.eye(P, dtype=np.float32),
        "decay": decay.reshape(P, -1).astype(np.float32),
        "lv_mask": mask.reshape(P, -1).view(np.int32),
        "inv_freq": np.tile(inv_freq.astype(np.float32)[None, :], (P, 1)),
    }


def layouts(i):
    def rows(w):
        lay, k, n = w.shape
        w = w.reshape(lay, k // P, P, n // COL, COL).transpose(0, 3, 2, 1, 4)
        return np.ascontiguousarray(w).reshape(lay, n // COL, P, k // P * COL)

    def gate_up(g, u):
        def half(w):
            return w.reshape(LAYERS, KD, P, FU, 256).transpose(0, 3, 2, 1, 4)
        return np.concatenate([half(g), half(u)], axis=-1).reshape(LAYERS, FU, P, KD * COL)

    w = i["w_in"]
    rq, rk, rv, rg, gq, gk, gv, ga, gg = np.split(w, np.cumsum([256, 256, 512, 512, 256, 256, 512, 16]), axis=-1)
    by_row = [i["ffn1_pre_g"], i["mix_pre_g"], i["xa_mem_g"], i["xa_pre_g"], i["ffn2_pre_g"],
              np.concatenate([i["ret_norm_g"], i["gla_norm_g"]], axis=1).reshape(LAYERS, D)]
    gains = np.stack(by_row, axis=1).reshape(LAYERS, N_GAINS, KD, P).transpose(3, 0, 1, 2)
    post = np.stack([i["ffn1_post_g"], i["mix_post_g"], i["xa_post_g"], i["ffn2_post_g"]], axis=1)
    arrays = {
        "x": i["x"].reshape(TOK, D), "mem": i["mem"].reshape(TOK, D),
        "positions": i["positions"].reshape(TT, P).T,
        "gu0": gate_up(i["ffn1_w_gate"], i["ffn1_w_up"]), "down0": rows(i["ffn1_w_down"]),
        "gu1": gate_up(i["ffn2_w_gate"], i["ffn2_w_up"]), "down1": rows(i["ffn2_w_down"]),
        "in": rows(np.concatenate([gq, gk, rq, rk, gv, rv, rg, gg], axis=-1)),
        "out": rows(i["w_out"]), "kv": rows(i["xa_w_kv"]), "q": rows(i["xa_w_q"]), "o": rows(i["xa_w_o"]),
        "w_ga": ga.reshape(LAYERS, KD, P, RANK).transpose(2, 0, 1, 3).reshape(P, -1),
        "w_a2": i["w_a2"].transpose(1, 0, 2).reshape(RANK, -1),
        "b_a2": i["b_a2"].reshape(LAYERS, 2, P).transpose(2, 0, 1).reshape(P, -1),
        "gains": gains.reshape(P, -1), "post_g": post.reshape(LAYERS * 4, D),
    }
    return {**arrays, **constants()}


def kernel(**inputs):
    import concourse.bacc as bacc
    from concourse.bass_utils import run_bass_kernel_spmd

    nc = bacc.Bacc("TRN2", target_bir_lowering=False, num_devices=1)
    arrays, aps = {}, {}
    for name, arr in layouts({k: np.asarray(v) for k, v in inputs.items()}).items():
        arrays[f"in_{name}"] = np.ascontiguousarray(arr)
        aps[name] = nc.dram_tensor(f"in_{name}", arr.shape, mybir.dt.from_np(arr.dtype), kind="ExternalInput").ap()
    out = nc.dram_tensor("out", (TOK, D), F32, kind="ExternalOutput").ap()
    program(nc, aps, out)
    r = run_bass_kernel_spmd(nc, [arrays], core_ids=[0])
    return r.results[0]["out"].reshape(1, TOK, D)
```

```python
from contextlib import ExitStack

import numpy as np

import concourse.bass as bass
from concourse import mybir

F32 = mybir.dt.float32
F32R = mybir.dt.float32r
BF16 = mybir.dt.bfloat16
I32 = mybir.dt.int32
I8 = mybir.dt.int8
ALU = mybir.AluOpType
ACT = mybir.ActivationFunctionType
AX = mybir.AxisListType
ds = bass.ds

P = 128
LAYERS = 2
D = 1024
TOK = 256
TT = TOK // P
KD = D // P
COL = 512
F = 2816
FU = F // (COL // 2)
KF = F // P
HEADS = 4
DK = 64
DV = 128
RANK = 16
XH = 4
EPS = 1e-6
TAU = 16.0

G_FFN1, G_MIX, G_MEM, G_XA, G_FFN2, G_HEAD = range(6)
N_GAINS = 6
DOWN = [(n, k, min(8, KF - k) // 2) for n in range(2) for k in range(0, KF, 8)]


def ffn_chunks(f):
    gain = (G_FFN1, G_FFN2)[f]
    up = [(f"gu{f}", j, 0, 4, gain) for j in range(FU)]
    return up + [(f"down{f}", n, k, nk, None) for n, k, nk in DOWN]


CHUNKS = ffn_chunks(0)
C_IN = len(CHUNKS)
CHUNKS += [("in", c, 0, 4, G_MIX) for c in range(6)]
C_OUT = len(CHUNKS)
CHUNKS += [("out", c, 0, 4, G_HEAD) for c in range(2)]
C_K = len(CHUNKS)
CHUNKS += [("kv", c, 0, 4, G_MEM) for c in range(2)]
C_Q = len(CHUNKS)
CHUNKS += [("q", c, 0, 4, G_XA) for c in range(2)]
C_V = len(CHUNKS)
CHUNKS += [("kv", 2 + c, 0, 4, G_MEM) for c in range(2)]
C_O = len(CHUNKS)
CHUNKS += [("o", c, 0, 4, None) for c in range(2)]
C_FFN2 = len(CHUNKS)
CHUNKS += ffn_chunks(1)
N_CH = len(CHUNKS)
C_FFN = (0, C_FFN2)
HALVES = 2 * N_CH
assert N_CH % 2 == 0
PAIRS = [c for f in range(2) for c in (C_FFN[f], C_FFN[f] + FU + 4)] + [C_IN, C_OUT, C_O]

Q_IN = FU + 2
Q_OUT = Q_IN + 6
Q_K = Q_OUT + 2
Q_Q = Q_K + 2
Q_V = Q_Q + 2
Q_AV = Q_V + 2
Q_O = Q_AV + 2
Q_FFN = (0, Q_O + 2)
N_Q = Q_FFN[1] + FU + 2
assert N_Q % 2 == 0
LAST_CHUNK = {Q_FFN[f] + j: C_FFN[f] + j for f in range(2) for j in range(FU)}
LAST_CHUNK.update({Q_FFN[f] + FU + n: C_FFN[f] + FU + 3 * n + 2 for f in range(2) for n in range(2)})
LAST_CHUNK.update({Q_IN + c: C_IN + c for c in range(6)})
for q0, c0, n in ((Q_OUT, C_OUT, 2), (Q_K, C_K, 2), (Q_Q, C_Q, 2), (Q_V, C_V, 2), (Q_O, C_O, 2)):
    LAST_CHUNK.update({q0 + c: c0 + c for c in range(n)})
PASSES = 2 * N_CH + XH

XUSE = [(t, a) for t in range(TT) for a in range(2)]
T_USES = [("x", 0, 1, 0), ("x", 0, 1, 1)] + [("h", 0, j) for j in range(FU)]
T_USES += [("x", 1, t, a) for t, a in XUSE]
T_USES += [("gqk", 0), ("gqk", 1), ("rqk", 0), ("rqk", 1)]
T_USES += [("mix", t, a) for t, a in XUSE]
T_USES += [("mem", t, a) for t, a in XUSE]
T_USES += [("x", 2, t, a) for t, a in XUSE]
T_USES += [("p", h) for h in range(XH)]
T_USES += [("x", 3, t, a) for t, a in XUSE]
T_USES += [("h", 1, j) for j in range(FU)]
T_USES += [("x", 4, 0, 0), ("x", 4, 0, 1)]
N_T = len(T_USES)
assert N_T % 2 == 0
SPLIT_USES = [u for u in T_USES if u[0] in ("x", "h", "mix", "mem")]
N_TS = len(SPLIT_USES)

LEVELS = [128, 64, 32, 16, 8, 4, 2, 1]
M_USES = ["z", "diag", "lv0", "lv1", "lv2", "rj0", "lv3", "rj1", "lv4", "lv5", "ro", "lv6", "lv7", "go",
          "s0", "s1"]
N_M = len(M_USES)
POOL_STEPS = 50


def program(nc, a, out):
    ctx = ExitStack()
    with ctx:
        def sb(name, shape, dt=F32, stack=ctx):
            return stack.enter_context(nc.sbuf_tensor(name, shape, dt))

        def sem(name):
            return ctx.enter_context(nc.semaphore(name))

        raw = sb("raw", [P, 4, 4, COL])
        w_hi = sb("w_hi", [P, 4, 4, COL], F32R)
        w_lo = sb("w_lo", [P, 4, 4, COL], F32R)
        x = sb("x", [P, TT, D])
        xT_hi = sb("xT_hi", [P, KD, TOK], F32R)
        xT_lo = sb("xT_lo", [P, KD, TOK], F32R)
        yg = sb("yg", [P, TT, D])
        post_gain = sb("post_gain", [P, D])
        ident = sb("ident", [P, P])
        ones = sb("ones", [P, P])
        decay = sb("decay", [P, 2, 2, TOK])
        lv_words = sb("lv_words", [P, 7 * 64 // 4], I32)
        lv_mask = lv_words[:, :].bitcast(I8).rearrange("p (v i) -> p v i", v=7)
        rope_c = sb("rope_c", [P, TT, DK])
        rope_s = sb("rope_s", [P, TT, DK])
        gains = sb("gains", [P, LAYERS * N_GAINS * KD])
        w_a2 = sb("w_a2", [RANK, LAYERS, 256])
        w_a2_l = sb("w_a2_l", [RANK, 256])
        b_a2 = sb("b_a2", [P, LAYERS * 2])
        w_ga = sb("w_ga", [P, LAYERS, KD, RANK])
        w_ga_s = sb("w_ga_s", [P, KD, RANK])
        w_ga_hi = sb("w_ga_hi", [P, KD, RANK], F32R)
        w_ga_lo = sb("w_ga_lo", [P, KD, RANK], F32R)
        junk_y = sb("junk_y", [P, COL], BF16)
        junk_x = sb("junk_x", [P, D], BF16)
        half_neg = sb("half_neg", [P, 8])
        yss = sb("yss", [P, TT, 2])
        xss = sb("xss", [P, TT])
        v_post = sb("v_post", [P, TT])
        r_post = sb("r_post", [P, TT])
        v_pre = sb("v_pre", [P, TT])
        r_pre = sb("r_pre", [P, TT])
        r_half = sb("r_half", [P, TT])
        c_half = sb("c_half", [P, TT])
        r_8 = sb("r_8", [P, TT])
        r_16 = sb("r_16", [P, TT])
        n_16 = sb("n_16", [P, TT])
        hss = sb("hss", [P, TT, 8])
        v_head = sb("v_head", [P, TT, 8])
        r_head = sb("r_head", [P, TT, 8])
        f_head = sb("f_head", [P, TT, 8])
        mss = sb("mss", [P, TT])
        v_mem = sb("v_mem", [P, TT])
        r_mem = sb("r_mem", [P, TT])
        smax = sb("smax", [P, XH, TT])
        nbias = sb("nbias", [P, XH, TT])
        rsum = sb("rsum", [P, XH, TT])
        rinv = sb("rinv", [P, XH, TT])
        gaT = sb("gaT", [RANK, TOK])

        with ExitStack() as region:
            hT_hi = sb("hT_hi", [P, KF, TOK], F32R, region)
            hT_lo = sb("hT_lo", [P, KF, TOK], F32R, region)
            h_tok = sb("h_tok", [P, 2, TT, 256], F32, region)
            th = sb("th", [P, TT, 256], F32, region)
            gt = sb("gt", [P, TT, 256], F32, region)
        with ExitStack() as region:
            o_sb = sb("o_sb", [P, TT, D], F32, region)
            gate = sb("gate", [P, TT, D], F32, region)
            v_tok = sb("v_tok", [P, TT, D], F32, region)
            gqk = sb("gqk", [P, TT, COL], F32, region)
            rqk = sb("rqk", [P, TT, COL], F32, region)
            gT = sb("gT", [P, 4, TOK], F32, region)
            rT = sb("rT", [P, 4, TOK], F32, region)
            pr0 = sb("pr0", [P, 2, 2, TOK], F32, region)
            pr1 = sb("pr1", [P, 2, 2, P], F32, region)
            pg = sb("pg", [P, 2, 4, P], F32, region)
            pgx = sb("pgx", [P, 2, 2, P], F32, region)
            rot_a = sb("rot_a", [P, COL], F32, region)
            rot_b = sb("rot_b", [P, COL], F32, region)
            cum = sb("cum", [P, 2, TOK], F32, region)
        zb = gate[:, 0, 0:COL].rearrange("p (r i) -> p r i", r=2)
        lg = gate[:, 0, COL:2 * COL].rearrange("p (r i) -> p r i", r=2)
        r_row = pr1[0:RANK, 0].rearrange("p r i -> p (r i)")
        dec = [o_sb[:, n, COL:2 * COL] for n in range(2)]
        av = [gqk[:, n, :] for n in range(2)]

        with ExitStack() as region:
            kT = sb("kT", [P, KD, TOK], F32, region)
            vx = sb("vx", [P, TT, D], F32, region)
            mem_t = sb("mem_t", [P, TT, D], F32, region)
            mT_hi = sb("mT_hi", [P, KD, TOK], F32R, region)
            mT_lo = sb("mT_lo", [P, KD, TOK], F32R, region)
            qT = sb("qT", [P, KD, TOK], F32, region)
            pr = sb("pr", [P, XH, TT, TOK], F32, region)
        pT = [mem_t[:, h // 2, h % 2 * COL:(h % 2 + 1) * COL].rearrange("p (m i) -> p m i", m=TT)
              for h in range(XH)]
        with ExitStack() as region:
            pos_i = sb("pos_i", [P, TT], I32, region)
            pos_f = sb("pos_f", [P, TT], F32, region)
            inv_f = sb("inv_f", [P, 32], F32, region)
            ang = sb("ang", [P, TT, 32], F32, region)
            turns = sb("turns", [P, TT, 32], F32, region)
            rest = [sb(f"rest{i}", [P, TT, 32], F32, region) for i in range(4)]
            absr = sb("absr", [P, TT, 32], F32, region)
            carg = sb("carg", [P, TT, 32], F32, region)
            sin_t = sb("sin_t", [P, TT, 32], F32, region)
            cos_t = sb("cos_t", [P, TT, 32], F32, region)

        acc = [[ctx.enter_context(nc.psum_tensor(f"acc{s}{t}", [P, COL], F32)) for t in range(TT)] for s in range(2)]
        tb = [ctx.enter_context(nc.psum_tensor(f"tb{i}", [P, COL], F32)) for i in range(2)]
        mb = [ctx.enter_context(nc.psum_tensor(f"mb{i}", [P, COL], F32)) for i in range(2)]

        s_const = sem("const_loaded")
        s_x_in = [sem(f"x_loaded{t}") for t in range(TT)]
        s_first = sem("identity_and_gains_loaded")
        s_pos = sem("positions_loaded")
        s_raw = [sem(f"raw_loaded{i}") for i in range(4)]
        s_gain = sem("post_gain_loaded")
        s_mem = sem("mem_loaded")
        s_out = sem("out_stored")
        s_hi = sem("w_hi_ready")
        s_lo = sem("w_lo_ready")
        s_half = sem("first_half_used")
        s_acc = sem("pass_done")
        s_accf = [sem(f"acc_free{i}") for i in range(4)]
        s_t = sem("transposed")
        s_thi = sem("transposed_hi_copied")
        s_tev = sem("transposed_evacuated")
        s_m = [sem(f"mixer_bank_done{i}") for i in range(2)]
        s_mf = [sem(f"mixer_bank_free{i}") for i in range(2)]
        s_ysq = sem("y_squared")
        s_xsq = sem("x_squared")
        s_rpost = sem("r_post_ready")
        s_rpre = sem("r_pre_ready")
        s_x = sem("x_ready")
        s_tanh = sem("tanh_ready")
        s_gated = sem("gate_scaled")
        s_pool = sem("pool_step")
        s_setup = sem("setup_step")
        s_trig = sem("sin_cos_ready")
        s_rope_t = sem("rope_table_ready")
        s_gas = sem("w_ga_scaled")
        s_gah = sem("w_ga_hi_ready")
        s_gal = sem("w_ga_lo_ready")
        s_a2 = sem("w_a2_ready")
        s_rrow = sem("r_row_ready")
        s_lsig = sem("log_sigmoid_step")
        s_la = sem("log_gate_ready")
        s_cum = sem("cum_ready")
        s_tmp = sem("exponent_ready")
        s_dec = sem("decay_ready")
        s_av = sem("decayed_qk_ready")
        s_rope = sem("rope_done")
        s_hss = sem("head_squares_summed")
        s_of = sem("heads_normed")
        s_gtanh = sem("mix_gate_tanh")
        s_mixed = sem("mixed_ready")
        s_msq = sem("mem_squared")
        s_rmem = sem("r_mem_ready")
        s_memn = sem("mem_normed")
        s_smax = sem("score_max_ready")
        s_nb = sem("exp_bias_ready")
        s_rinv = sem("row_sum_inverted")
        s_p = sem("probs_ready")
        s_ohi = sem("attention_hi_copied")

        def half_no(l, ci, h):
            return l * HALVES + 2 * ci + h

        def pieces(nk):
            return ((0, 2), (2, nk))

        def t_no(l, use):
            if use[0] == "x" and use[1:3] == (0, 0):
                return l * N_T + use[3]
            return l * N_T + T_USES.index(use) + 2

        def t_bank(use):
            return (use[3] if use[:3] == ("x", 0, 0) else T_USES.index(use)) % 2

        def ts_no(l, use):
            if use[0] == "x" and use[1:3] == (0, 0):
                return l * N_TS + use[3]
            return l * N_TS + SPLIT_USES.index(use) + 2

        def m_no(l, use):
            return l * N_M + M_USES.index(use) + 1

        def chunk_pass_no(l, ci, t):
            if ci in PAIRS:
                at = 2 * t
            elif ci - 1 in PAIRS:
                at = 2 * t - 1
            else:
                at = t
            return l * PASSES + 2 * ci + at + (XH if ci >= C_O else 0) + 1

        def pass_no(l, q, t):
            if Q_AV <= q < Q_O:
                return l * PASSES + 2 * C_O + 2 * (q - Q_AV) + t + 1
            return chunk_pass_no(l, LAST_CHUNK[q], t)

        def acc_uses(l, q):
            return l * (N_Q // 2) + q // 2 + 1

        def y_no(l, phase, n, t):
            return l * 16 + 4 * phase + (2 * t + n if phase in (1, 2) else 2 * n + t)

        def gated_no(l, f, j, t, i=None):
            at = 2 * t + j if j < 2 else 2 * j + t
            return l * 4 * FU + f * 2 * FU + at + (0 if i is None else i * 4)

        def bank(q, t):
            return 2 * (q % 2) + t

        def other(l):
            return l * -1 + 1

        def weight_src(ci, h, l, j=None):
            lay = l
            if ci >= N_CH:
                ci, lay = ci - N_CH, other(l)
            name, col, k0, nk, _ = CHUNKS[ci]
            w = a[name]
            col = col if j is None else j
            n_cols = w.shape[1]
            flat = w.rearrange("l c p k -> (l c) p k")
            src = flat[ds(lay * n_cols + col, 1), :, (k0 + h * nk) * COL:(k0 + h * nk + nk) * COL]
            return src.rearrange("o p k -> (o p) k"), nk

        block = ctx.enter_context(nc.Block())

        @block.sync
        def _(sp):
            def load(l, ci, j=None, extra=0, halves=(0, 1)):
                for h in halves:
                    slot = (2 * ci + h) % 4
                    src, nk = weight_src(ci, h, l, j)
                    if not isinstance(l, int):
                        sp.wait_ge(s_lo, 4 * half_no(l, ci, h) + 4 * extra - 12)
                    sp.dma_start(raw[:, slot, 0:nk, :].rearrange("p k n -> p (k n)"), src).then_inc(s_raw[slot], 16)

            def load_post_gain(l, phase):
                q_last = {0: Q_FFN[0] + FU + 1, 1: Q_OUT + 1, 2: Q_O + 1, 3: Q_FFN[1] + FU + 1}
                prev = q_last[(phase - 1) % 4]
                sp.wait_ge(s_accf[bank(prev, 1)], acc_uses(l, prev) + 1 - (N_Q // 2 if phase == 0 else 0))
                src = a["post_g"][ds(l * 4 + phase, 1), :]
                sp.dma_start(post_gain[:, :], src.to_broadcast([P, D])).then_inc(s_gain, 16)

            sp.dma_start(ident[:, :], a["ident"]).then_inc(s_first, 16)
            sp.dma_start(x[:, 0, :], a["x"][0:P, :]).then_inc(s_x_in[0], 16)
            sp.dma_start(gains[:, :], a["gains"]).then_inc(s_first, 16)
            load(0, 0)
            sp.dma_start(x[:, 1, :], a["x"][P:2 * P, :]).then_inc(s_x_in[1], 16)
            load(0, 1)
            for dst, name in ((decay[:, :, :, :].rearrange("p e r i -> p (e r i)"), "decay"),
                              (lv_words[:, :], "lv_mask"),
                              (w_a2[:, :, :].rearrange("r l n -> r (l n)"), "w_a2"), (b_a2[:, :], "b_a2"),
                              (w_ga[:, :, :, :].rearrange("p l k n -> p (l k n)"), "w_ga")):
                sp.dma_start(dst, a[name]).then_inc(s_const, 16)

            def ffn_loads(l, f):
                c0 = C_FFN[f]
                with sp.Fori(0, (FU - 3) // 2) as i:
                    for p in range(2):
                        load(l, c0 + 2 + p, j=i * 2 + 2 + p, extra=i * 4)
                load(l, c0 + FU - 1)
                for ci in range(c0 + FU, c0 + FU + 6):
                    if ci == c0 + FU + 1:
                        load_post_gain(l, (0, 3)[f])
                    load(l, ci)

            with sp.Fori(0, LAYERS) as l:
                ffn_loads(l, 0)
                for ci in range(C_IN, C_FFN2 + 2):
                    if ci == C_IN + 4:
                        load_post_gain(l, 1)
                    if ci == C_K:
                        sp.wait_ge(s_of, l * 4 + 4)
                        sp.dma_start(mem_t[:, :, :], a["mem"].rearrange("(t p) d -> p t d", p=P)).then_inc(s_mem, 16)
                    if ci == C_K + 3:
                        load_post_gain(l, 2)
                    load(l, ci)
                ffn_loads(l, 1)
                load(l, N_CH)
                load(l, N_CH + 1)
            for t in range(TT):
                sp.wait_ge(s_x, 4 + 16 * (LAYERS - 1) + 12 + 2 * t + 2)
                sp.dma_start(out[t * P:(t + 1) * P, :], x[:, t, :]).then_inc(s_out, 16)
            for s in range(4):
                sp.wait_ge(s_raw[s], 16 * (LAYERS * HALVES // 4 + 1))
            sp.wait_ge(s_out, 16 * TT)

        @block.tensor
        def _(pe):
            def wait_acc(l, q, t, extra=0):
                pe.wait_ge(s_accf[bank(q, t)], acc_uses(l, q) + extra)

            def wait_split(use, l):
                pe.wait_ge(s_tev, t_no(l, use) + 1)

            def three(o, st_hi, st_lo, mv_hi, mv_lo, first, last):
                pe.matmul(o, st_hi, mv_hi, start=first, stop=False)
                pe.matmul(o, st_hi, mv_lo, start=False, stop=False)
                return pe.matmul(o, st_lo, mv_hi, start=False, stop=last)

            def token_pass(l, ci, q, t, src_hi, src_lo, k_src=0, first=True, last=True, x_ci=0, x_q=0,
                           mid=None, before_k=None):
                nk, gained = CHUNKS[ci % N_CH][3], CHUNKS[ci % N_CH][4] is not None
                if first:
                    wait_acc(l, q, t, x_q)
                o = acc[q % 2][t]
                for h in range(2):
                    slot = (2 * ci + h) % 4
                    if h == 1 and mid is not None:
                        mid()
                    for k in range(nk):
                        if t == 0 and (gained or k in (0, 2)):
                            step = k + 1 if gained else k + 2
                            pe.wait_ge(s_lo, 4 * half_no(l, ci, h) + 4 * x_ci + step)
                        ks = k_src + h * nk + k
                        if before_k is not None:
                            before_k(ks)
                        sl = slice(t * P, t * P + P)
                        mm = three(o[:, :], src_hi[:, ks, sl], src_lo[:, ks, sl], w_hi[:, slot, k, :],
                                   w_lo[:, slot, k, :], first and h == 0 and k == 0, last and h == 1 and k == nk - 1)
                        if t == 1 and k == nk - 1 and h == 0:
                            mm.then_inc(s_half, 1)
                return mm

            def chunk_pass(l, ci, q, t, src_hi, src_lo, **kw):
                token_pass(l, ci, q, t, src_hi, src_lo, **kw).then_inc(s_acc, 1)

            def column_pass(l, ci, q, t, src_hi, src_lo):
                wait_acc(l, q, t)
                for mt in range(2):
                    c = (2 * t + mt) * P
                    for h in range(2):
                        slot = (2 * ci + h) % 4
                        for k in range(4):
                            if t == 0 and mt == 0:
                                pe.wait_ge(s_lo, 4 * half_no(l, ci, h) + k + 1)
                            mm = three(acc[q % 2][t][:, mt * 256:mt * 256 + 256], w_hi[:, slot, k, c:c + P],
                                       w_lo[:, slot, k, c:c + P], src_hi[:, 4 * h + k, :], src_lo[:, 4 * h + k, :],
                                       h == 0 and k == 0, h == 1 and k == 3)
                        if t == 1 and mt == 1 and h == 0:
                            mm.then_inc(s_half, 1)
                mm.then_inc(s_acc, 1)

            def transposes(l, use, pieces, extra=0):
                n = t_no(l, use)
                if use[:3] != ("x", 0, 0):
                    pe.wait_ge(s_tev, n - 1 + extra)
                for (lo, w), src in pieces:
                    rows = src.shape[1]
                    mm = pe.transpose(tb[t_bank(use)][0:rows, lo:lo + w], src, ident[:, :])
                mm.then_inc(s_t, 1)

            def x_transposes(l, phase, t):
                for half in range(2):
                    pe.wait_ge(s_x, l * 16 + 4 * phase + 2 * t + half + 1)
                    transposes(l, ("x", phase, t, half),
                               [((k * P, P), x[:, t, (4 * half + k) * P:(4 * half + k + 1) * P]) for k in range(4)])

            def wait_x(l, phase, t):
                wait_split(("x", phase, t, 1), l)

            def h_transposes(l, f, j, i=0):
                q = Q_FFN[f] + j
                for t in range(TT):
                    pe.wait_ge(s_accf[bank(q, t)], acc_uses(l, q) + 1 + i)
                transposes(l, ("h", f, j), [(((2 * c + t) * P, P), h_tok[:, j % 2, t, c * P:(c + 1) * P])
                                            for c in range(2) for t in range(TT)], extra=i * 2)

            def pair(l, ci, q, src, k_src=(0, 0), first=(True, True), last=(True, True), wait_tile=None,
                     mids=None, before_k=None, before_last=None):
                for t in range(TT):
                    for n in range(2):
                        if t == 1 and n == 1 and before_last is not None:
                            before_last()
                        if n == 0 and wait_tile is not None:
                            wait_tile(t)
                        chunk_pass(l, ci + n, q[n], t, *src, k_src=k_src[n], first=first[n], last=last[n],
                                   mid=(mids or {}).get(2 * t + n), before_k=(before_k or {}).get(2 * t + n))

            def ffn(l, f):
                c0, q0, phase = C_FFN[f], Q_FFN[f], (0, 3)[f]

                def up(j, i=0):
                    for t in range(TT):
                        chunk_pass(l, c0 + j, q0 + j, t, xT_hi, xT_lo, x_ci=i * 4, x_q=i)
                        if t == 0:
                            h_transposes(l, f, j - 1, i)
                pair(l, c0, (q0, q0 + 1), (xT_hi, xT_lo), wait_tile=lambda t: wait_x(l, phase, t),
                     mids={1: lambda: x_transposes(l, phase, 1)})
                h_transposes(l, f, 0)
                with pe.Fori(0, (FU - 5) // 2) as i:
                    for p in range(2):
                        up(2 + p, i)
                for j in range(FU - 3, FU):
                    up(j)
                for d, (n, k0, nk) in enumerate(DOWN[:4]):
                    for t in range(TT):
                        if n == 0 and k0 == 0 and t == 0:
                            wait_split(("h", f, FU - 2), l)
                        if n == 0 and k0 + 2 * nk == KF:
                            wait_split(("h", f, FU - 1), l)
                        chunk_pass(l, c0 + FU + d, q0 + FU + n, t, hT_hi, hT_lo, k_src=k0, first=k0 == 0,
                                   last=k0 + 2 * nk == KF)
                        if d == 0 and t == 0:
                            h_transposes(l, f, FU - 1)
                pair(l, c0 + FU + 4, (q0 + FU + 1,) * 2, (hT_hi, hT_lo), k_src=(DOWN[4][1], DOWN[5][1]),
                     first=(False, False), last=(False, True), before_last=lambda: x_transposes(l, phase + 1, 0))

            def wait_m(l, use, e):
                pe.wait_ge(s_mf[e], m_no(l, use))

            def level(l, n):
                b = LEVELS[n]
                pe.wait_ge(s_av, l * 8 + n + 1)
                A = av[n % 2].rearrange("p (r i) -> p r i", r=2)
                for e in range(2):
                    wait_m(l, f"lv{n}", e)
                    rows = slice(64 * e, 64 * e + 64)
                    if b == P:
                        for r in range(2):
                            mm = pe.matmul(mb[e][:, r * P:(r + 1) * P], A[rows, r, 0:P], A[rows, r, P:2 * P],
                                           start=True, stop=True)
                    else:
                        for t in range(TT):
                            for r in range(2):
                                tile = A[rows, r, t * P:(t + 1) * P]
                                later = tile.rearrange("p (g two b) -> p g two b", two=2, b=b)[:, :, 1, :]
                                c = (2 * t + r) * 64
                                mm = pe.matmul(mb[e][:, c:c + 64], tile, later, start=True, stop=True)
                    mm.then_inc(s_m[e], 1)

            def mixed_transposes(l, t, groups=(0, 1)):
                for g in groups:
                    pe.wait_ge(s_mixed, l * 4 + 2 * g + t + 1)
                    transposes(l, ("mix", t, g), [((k * P, P), o_sb[:, t, (4 * g + k) * P:(4 * g + k + 1) * P])
                                                  for k in range(4)])

            def mixer(l):
                def after(k):
                    if k == 1:
                        pe.wait_ge(s_gal, l + 1)
                        wait_m(l, "z", 0)
                        for kt in range(KD):
                            three(mb[0][0:RANK, 0:TOK], w_ga_hi[:, kt, :], w_ga_lo[:, kt, :], xT_hi[:, kt, :],
                                  xT_lo[:, kt, :], kt == 0, kt == KD - 1)
                        pe.wait_ge(s_rpre, l * 8 + 2 + 1 + 1)
                        for t in range(TT):
                            mm = pe.matmul(mb[0][0:RANK, TOK + t * P:TOK + (t + 1) * P],
                                           r_pre[:, t:t + 1].to_broadcast([P, RANK]), ident[:, :], start=True, stop=True)
                        mm.then_inc(s_m[0], 1)
                    if k == 3:
                        pe.wait_ge(s_mf[0], m_no(l, "z") + 1)
                        pe.wait_ge(s_a2, l + 1)
                        wait_m(l, "z", 1)
                        for r in range(2):
                            mm = pe.matmul(mb[1][:, r * TOK:(r + 1) * TOK], w_a2_l[:, r * P:(r + 1) * P], gaT[:, :],
                                           start=True, stop=True)
                        mm.then_inc(s_m[1], 1)
                        for t in range(TT):
                            pe.wait_ge(s_accf[bank(Q_IN, t)], acc_uses(l, Q_IN) + 1)
                            transposes(l, ("gqk", t), [((g * P, P), gqk[:, t, g * P:(g + 1) * P]) for g in range(4)])
                    if k == "in 4":
                        wait_split(("gqk", 1), l)
                        for e in range(2):
                            wait_m(l, "diag", e)
                            rows = slice(64 * e, 64 * e + 64)
                            for t in range(TT):
                                for r in range(2):
                                    c = (2 * t + r) * P
                                    mm = pe.matmul(mb[e][:, c:c + P], gT[rows, 2 + r, t * P:(t + 1) * P],
                                                   gT[rows, r, t * P:(t + 1) * P], start=True, stop=True)
                            mm.then_inc(s_m[e], 1)
                    if k == "in 5":
                        level(l, 0)
                    if k == 5:
                        level(l, 1)
                        for t in range(TT):
                            pe.wait_ge(s_rope, l * 2 + t + 1)
                            transposes(l, ("rqk", t), [((g * P, P), rqk[:, t, g * P:(g + 1) * P]) for g in range(4)])
                    if k == 6:
                        level(l, 2)
                    if k == "in 7":
                        wait_split(("rqk", 1), l)
                        for e in range(2):
                            wait_m(l, "rj0", e)
                            rows = slice(64 * e, 64 * e + 64)
                            for r in range(2):
                                mm = pe.matmul(mb[e][:, r * TOK:(r + 1) * TOK], rT[rows, 2 + r, 0:P], rT[rows, r, :],
                                               start=True, stop=True)
                            mm.then_inc(s_m[e], 1)
                    if k == 7:
                        level(l, 3)
                    if k == "in 8":
                        for e in range(2):
                            wait_m(l, "rj1", e)
                            rows = slice(64 * e, 64 * e + 64)
                            for r in range(2):
                                mm = pe.matmul(mb[e][:, r * P:(r + 1) * P], rT[rows, 2 + r, P:2 * P],
                                               rT[rows, r, P:2 * P], start=True, stop=True)
                            mm.then_inc(s_m[e], 1)
                    if k == 8:
                        level(l, 4)
                        level(l, 5)
                        for t in range(TT):
                            pe.wait_ge(s_accf[bank(Q_IN + 3, t)], acc_uses(l, Q_IN + 3) + 1)
                        for t in range(TT):
                            wait_m(l, "ro", t)
                            for hd in range(HEADS):
                                r, e = hd // 2, hd % 2
                                o = mb[t][:, hd * DV:(hd + 1) * DV]
                                v0 = v_tok[:, 0, hd * DV:(hd + 1) * DV]
                                mm = pe.matmul(o, pr0[:, e, r, t * P:(t + 1) * P], v0, start=True, stop=t == 0)
                                if t == 1:
                                    mm = pe.matmul(o, pr1[:, e, r, :], v_tok[:, 1, hd * DV:(hd + 1) * DV],
                                                   start=False, stop=True)
                            mm.then_inc(s_m[t], 1)
                    if k == 9:
                        level(l, 6)
                        level(l, 7)
                    if k == "in 11":
                        mixed_transposes(l, 0, (0,))
                    if k == "in 10":
                        for t in range(TT):
                            pe.wait_ge(s_accf[bank(Q_IN + 2, t)], acc_uses(l, Q_IN + 2) + 1)
                        for t in range(TT):
                            wait_m(l, "go", 0)
                            wait_m(l, "go", 1)
                            for hd in range(HEADS):
                                r, e = hd // 2, hd % 2
                                o = mb[t][:, hd * DV:(hd + 1) * DV]
                                c = COL + hd * DV
                                if t == 0:
                                    mm = pe.matmul(o, pg[:, e, r, :], v_tok[:, 0, c:c + DV], start=True, stop=True)
                                else:
                                    pe.matmul(o, pgx[:, e, r, :], v_tok[:, 0, c:c + DV], start=True, stop=False)
                                    mm = pe.matmul(o, pg[:, e, 2 + r, :], v_tok[:, 1, c:c + DV], start=False, stop=True)
                            mm.then_inc(s_m[t], 1)

                pair(l, C_IN, (Q_IN, Q_IN + 1), (xT_hi, xT_lo), wait_tile=lambda t: wait_x(l, 1, t),
                     mids={1: lambda: x_transposes(l, 1, 1)}, before_last=lambda: after(1))
                after(3)
                for k in range(4, 12):
                    c, t = k // 2, k % 2
                    chunk_pass(l, C_IN + c, Q_IN + c, t, xT_hi, xT_lo, mid=lambda: after(f"in {k}"))
                    after(k)

            def mem_transposes(l, t):
                pe.wait_ge(s_memn, l * 2 + t + 1)
                for g in range(2):
                    transposes(l, ("mem", t, g), [((k * P, P), mem_t[:, t, (4 * g + k) * P:(4 * g + k + 1) * P])
                                                  for k in range(4)])

            def scores(l, h):
                bk = h % 2
                use = "s0" if h < 2 else "s1"
                wait_m(l, use, bk)
                for t in range(TT):
                    for kk in range(2):
                        mm = pe.matmul(mb[bk][:, t * TOK:(t + 1) * TOK], qT[:, 2 * h + kk, t * P:(t + 1) * P],
                                       kT[:, 2 * h + kk, :], start=kk == 0, stop=kk == 1)
                mm.then_inc(s_m[bk], 1)

            def prob_transposes(l, h):
                pe.wait_ge(s_p, l * XH + h + 1)
                transposes(l, ("p", h), [(((2 * m + t) * P, P), pr[:, h, t, m * P:(m + 1) * P])
                                         for m in range(2) for t in range(TT)])

            def attend(l, h):
                q, t = Q_AV + h // 2, h % 2
                wait_acc(l, q, t)
                wait_split(("p", h), l)
                for dv in range(2):
                    c = h * 256 + dv * P
                    for m in range(2):
                        mm = pe.matmul(acc[q % 2][t][:, dv * TOK:(dv + 1) * TOK], vx[:, m, c:c + P],
                                       pT[h][:, m, :], start=m == 0, stop=m == 1)
                mm.then_inc(s_acc, 1)

            pe.wait_ge(s_first, 32)
            x_transposes(0, 0, 0)
            with pe.Fori(0, LAYERS) as l:
                ffn(l, 0)
                mixer(l)
                mixed_transposes(l, 0, (1,))

                def mix_split(t):
                    def wait(ks):
                        if ks % 4 == 0:
                            wait_split(("mix", t, ks // 4), l)
                    return wait
                pair(l, C_OUT, (Q_OUT, Q_OUT + 1), (xT_hi, xT_lo), before_k={0: mix_split(0), 2: mix_split(1)},
                     mids={0: lambda: mixed_transposes(l, 1), 1: lambda: mem_transposes(l, 0),
                           2: lambda: mem_transposes(l, 1)})
                wait_split(("mem", 1, 1), l)
                for t in range(TT):
                    column_pass(l, C_K, Q_K, t, mT_hi, mT_lo)
                    x_transposes(l, 2, t)
                for t in range(TT):
                    column_pass(l, C_K + 1, Q_K + 1, t, mT_hi, mT_lo)
                wait_x(l, 2, 1)
                column_pass(l, C_Q, Q_Q, 0, xT_hi, xT_lo)
                column_pass(l, C_Q, Q_Q, 1, xT_hi, xT_lo)
                column_pass(l, C_Q + 1, Q_Q + 1, 0, xT_hi, xT_lo)
                for t in range(TT):
                    for q in (Q_K, Q_K + 1, Q_Q):
                        pe.wait_ge(s_accf[bank(q, t)], acc_uses(l, q) + 1)
                scores(l, 0)
                scores(l, 1)
                column_pass(l, C_Q + 1, Q_Q + 1, 1, xT_hi, xT_lo)
                chunk_pass(l, C_V, Q_V, 0, mT_hi, mT_lo)
                pe.wait_ge(s_accf[bank(Q_Q + 1, 0)], acc_uses(l, Q_Q + 1) + 1)
                scores(l, 2)
                chunk_pass(l, C_V, Q_V, 1, mT_hi, mT_lo)
                pe.wait_ge(s_accf[bank(Q_Q + 1, 1)], acc_uses(l, Q_Q + 1) + 1)
                scores(l, 3)
                prob_transposes(l, 0)
                prob_transposes(l, 1)
                chunk_pass(l, C_V + 1, Q_V + 1, 0, mT_hi, mT_lo)
                prob_transposes(l, 2)
                chunk_pass(l, C_V + 1, Q_V + 1, 1, mT_hi, mT_lo)
                prob_transposes(l, 3)
                for h in range(XH):
                    for t in range(TT):
                        q = Q_V + h // 2
                        pe.wait_ge(s_accf[bank(q, t)], acc_uses(l, q) + 1)
                    attend(l, h)

                def head_split(ks):
                    if ks % 2 == 0:
                        q, t = Q_AV + ks // 4, ks // 2 % 2
                        pe.wait_ge(s_accf[bank(q, t)], acc_uses(l, q) + 1)
                pair(l, C_O, (Q_O, Q_O + 1), (xT_hi, xT_lo), before_k={0: head_split},
                     before_last=lambda: x_transposes(l, 3, 0))
                ffn(l, 1)

        @block.scalar
        def _(act):
            def split_hi(l, ci, h, i=None):
                lay = l
                if ci >= N_CH:
                    lay = other(l)
                _, _, _, nk, gain = CHUNKS[ci % N_CH]
                slot = (2 * ci + h) % 4
                x4 = 0 if i is None else i * 4
                x1 = 0 if i is None else i
                act.wait_ge(s_raw[slot], (l * (HALVES // 4) + x1 + (2 * ci + h) // 4 + 1) * 16)
                if h == 0:
                    act.wait_ge(s_half, l * N_CH + ci + x1 * 2)
                elif ci == 1:
                    act.wait_ge(s_acc, l * PASSES + 1)
                else:
                    act.wait_ge(s_acc, chunk_pass_no(l, ci - 2, 1) + 1 + x4)
                if gain is None:
                    for a, b in pieces(nk):
                        act.activation(w_hi[:, slot, a:b, :], raw[:, slot, a:b, :], ACT.Copy).then_inc(s_hi, 2)
                    return
                act.nop(nofuse=True)
                for k in range(nk):
                    g = lay * (N_GAINS * KD) + gain * KD + h * nk + k
                    act.activation(w_hi[:, slot, k, :], raw[:, slot, k, :], ACT.Copy,
                                   scale=gains[:, ds(g, 1)]).then_inc(s_hi, 1)

            def wait_pass(l, q, t, i=0):
                act.wait_ge(s_acc, pass_no(l, q, t) + 1 + i * 4)

            def t_hi(l, use, dst, cols=COL, extra=0):
                act.wait_ge(s_t, t_no(l, use) + 1 + extra)
                act.activation(dst, tb[t_bank(use)][:, 0:cols], ACT.Copy).then_inc(s_thi, 1)

            def x_hi(l, phase, t):
                for g in range(2):
                    t_hi(l, ("x", phase, t, g), xT_hi[:, 4 * g:4 * g + 4, t * P:(t + 1) * P])

            def x_square(l, phase, t):
                for half in range(2):
                    act.wait_ge(s_x, l * 16 + 4 * phase + 2 * t + half + 1)
                if not (phase == 0 and t == 0):
                    act.wait_ge(s_xsq, l * 8 + 2 * phase + t)
                act.activation(junk_x[:, :], x[:, t, :], ACT.Square, accum_out=xss[:, t:t + 1]).then_inc(s_xsq, 1)

            def y_square(l, phase, q, n, t):
                wait_pass(l, q, t)
                if (phase, n, t) != (0, 0, 0):
                    act.wait_ge(s_ysq, y_no(l, phase, n, t))
                act.activation(junk_y[:, :], acc[q % 2][t][:, :], ACT.Square,
                               accum_out=yss[:, t, n:n + 1]).then_inc(s_ysq, 1)

            def boundary(l, phase, q, ci):
                y_square(l, phase, q, 1, 0)
                split_hi(l, ci + 1, 0)
                x_hi(l, phase + 1, 0)
                x_square(l, phase + 1, 0)
                if phase == 2:
                    y_square(l, phase, q - 1, 0, 1)
                split_hi(l, ci + 1, 1)
                y_square(l, phase, q, 1, 1)
                split_hi(l, ci + 2, 0)

            def ffn(l, f):
                c0, q0, phase = C_FFN[f], Q_FFN[f], (0, 3)[f]
                split_hi(l, c0 + 1, 1)
                x_hi(l, phase, 1)
                x_square(l, phase, 1)

                def h_hi(j, i):
                    if i is None:
                        dst = hT_hi[:, 2 * j:2 * j + 2, :]
                    else:
                        dst = hT_hi[:, ds(i * 4 + 2 * j, 2), :]
                    t_hi(l, ("h", f, j), dst, extra=0 if i is None else i * 2)

                def tanh(j, t, i):
                    x1 = 0 if i is None else i
                    wait_pass(l, q0 + j, t, x1)
                    if j == 0:
                        act.wait_ge(s_rpre, l * 8 + 2 * phase + t + 1)
                    elif j == 1:
                        act.wait_ge(s_gated, gated_no(l, f, 0, t) + 1)
                    else:
                        act.wait_ge(s_gated, l * 4 * FU + f * 2 * FU + 2 * j + t - 1 + x1 * 4)
                    act.activation(th[:, t, :], acc[(q0 + j) % 2][t][:, 0:256], ACT.Tanh,
                                   scale=r_half[:, t:t + 1]).then_inc(s_tanh, 1)

                def up(j, i=None):
                    tanh(j, 0, i)
                    h_hi(j - 1, i)
                    split_hi(l, c0 + j + 1, 1, i)
                    tanh(j, 1, i)
                    split_hi(l, c0 + j + 2, 0, i)
                tanh(0, 0, None)
                tanh(1, 0, None)
                split_hi(l, c0 + 2, 0)
                tanh(0, 1, None)
                split_hi(l, c0 + 2, 1)
                tanh(1, 1, None)
                h_hi(0, None)
                split_hi(l, c0 + 3, 0)
                with act.Fori(0, (FU - 5) // 2) as i:
                    for p in range(2):
                        up(2 + p, i)
                for j in range(FU - 3, FU):
                    up(j)
                for d in range(6):
                    ci = c0 + FU + d
                    if d == 0:
                        h_hi(FU - 1, None)
                    if d == 3:
                        y_square(l, phase, q0 + FU, 0, 0)
                        y_square(l, phase, q0 + FU, 0, 1)
                    if d < 5:
                        split_hi(l, ci + 1, 1)
                    if d < 4:
                        split_hi(l, ci + 2, 0)
                boundary(l, phase, q0 + FU + 1, c0 + FU + 5)

            def exp_decay(l, n):
                act.wait_ge(s_tmp, l * 8 + n + 1)
                act.activation(dec[n % 2], dec[n % 2], ACT.Exp, scale=1.0 / TAU).then_inc(s_dec, 1)

            def head_outputs(l, use, g):
                for t in range(TT):
                    act.wait_ge(s_m[t], m_no(l, use) + 1)
                    if g == 1:
                        act.wait_ge(s_hss, l * 4 + t + 1)
                    sq = (rot_a, rot_b)[t]
                    act.activation(sq[:, :], mb[t][:, :], ACT.Square)
                    act.activation(o_sb[:, t, g * COL:(g + 1) * COL], mb[t][:, :], ACT.Copy).then_inc(s_mf[t], 1)

            def mixer(l):
                def project(c, t, dst, scale):
                    wait_pass(l, Q_IN + c, t)
                    act.activation(dst, acc[(Q_IN + c) % 2][t][:, :], ACT.Copy,
                                   scale=scale[:, t:t + 1]).then_inc(s_accf[bank(Q_IN + c, t)], 1)

                def gate_tanh(c, t):
                    wait_pass(l, Q_IN + c, t)
                    g = c - 4
                    act.activation(gate[:, t, g * COL:(g + 1) * COL], acc[(Q_IN + c) % 2][t][:, :], ACT.Tanh,
                                   scale=r_half[:, t:t + 1]).then_inc(s_gtanh, 1)

                def split_after(k):
                    ci = C_IN + k // 2
                    if k % 2 == 0:
                        split_hi(l, ci + 1, 1)
                    else:
                        split_hi(l, ci + 2, 0)
                act.wait_ge(s_gas, l + 1)
                act.activation(w_ga_hi[:, :, :], w_ga_s[:, :, :], ACT.Copy).then_inc(s_gah, 1)
                split_hi(l, C_IN + 1, 1)
                x_hi(l, 1, 1)
                x_square(l, 1, 1)
                act.wait_ge(s_rpre, l * 8 + 2 + 0 + 1)
                project(0, 0, gqk[:, 0, :], r_pre)
                project(1, 0, rqk[:, 0, :], r_pre)
                split_hi(l, C_IN + 2, 0)
                act.wait_ge(s_rpre, l * 8 + 2 + 1 + 1)
                project(0, 1, gqk[:, 1, :], r_pre)
                split_hi(l, C_IN + 2, 1)
                project(1, 1, rqk[:, 1, :], r_pre)
                act.wait_ge(s_mf[1], m_no(l, "z") + 1)
                act.activation(lg, zb, ACT.Abs).then_inc(s_lsig, 1)
                act.wait_ge(s_lsig, l * 3 + 1)
                act.activation(lg, lg, ACT.Exp, scale=-1.0).then_inc(s_lsig, 1)
                act.wait_ge(s_lsig, l * 3 + 2)
                act.activation(lg, lg, ACT.Ln, bias=1.0).then_inc(s_lsig, 1)
                split_after(3)
                exp_decay(l, 0)
                exp_decay(l, 1)
                project(2, 0, v_tok[:, 0, COL:2 * COL], r_8)
                split_after(4)
                exp_decay(l, 2)
                exp_decay(l, 3)
                project(2, 1, v_tok[:, 1, COL:2 * COL], r_8)
                split_after(5)
                exp_decay(l, 4)
                project(3, 0, v_tok[:, 0, 0:COL], r_pre)
                split_after(6)
                exp_decay(l, 5)
                project(3, 1, v_tok[:, 1, 0:COL], r_pre)
                split_after(7)
                exp_decay(l, 6)
                gate_tanh(4, 0)
                split_after(8)
                exp_decay(l, 7)
                head_outputs(l, "ro", 0)
                gate_tanh(4, 1)
                split_after(9)
                head_outputs(l, "go", 1)
                gate_tanh(5, 0)
                split_after(10)

                def mix_hi(t):
                    for g in range(2):
                        t_hi(l, ("mix", t, g), xT_hi[:, 4 * g:4 * g + 4, t * P:(t + 1) * P])
                mix_hi(0)
                gate_tanh(5, 1)
                split_after(11)
                mix_hi(1)
                split_hi(l, C_OUT + 1, 1)

            def mem_hi(l, t):
                for g in range(2):
                    t_hi(l, ("mem", t, g), mT_hi[:, 4 * g:4 * g + 4, t * P:(t + 1) * P])

            def mix_out(l):
                act.wait_ge(s_mem, l * 16 + 16)
                for t in range(TT):
                    if t == 1:
                        act.wait_ge(s_msq, l * 2 + 1)
                    else:
                        act.wait_ge(s_xsq, l * 8 + 4)
                    act.activation(junk_x[:, :], mem_t[:, t, :], ACT.Square,
                                   accum_out=mss[:, t:t + 1]).then_inc(s_msq, 1)
                y_square(l, 1, Q_OUT, 0, 0)
                mem_hi(l, 0)
                y_square(l, 1, Q_OUT + 1, 1, 0)
                split_hi(l, C_OUT + 2, 0)
                mem_hi(l, 1)
                act.wait_ge(s_msq, l * 2 + 2)
                x_square(l, 2, 0)
                y_square(l, 1, Q_OUT, 0, 1)
                split_hi(l, C_OUT + 2, 1)
                y_square(l, 1, Q_OUT + 1, 1, 1)
                split_hi(l, C_K + 1, 0)

            def attention(l):
                def copy_out(q, t, dst):
                    wait_pass(l, q, t)
                    act.activation(dst, acc[q % 2][t][:, :], ACT.Copy).then_inc(s_accf[bank(q, t)], 1)
                x_hi(l, 2, 0)
                copy_out(Q_K, 0, kT[:, 0:2, :])
                split_hi(l, C_K + 1, 1)
                x_hi(l, 2, 1)
                copy_out(Q_K, 1, kT[:, 2:4, :])
                x_square(l, 2, 1)
                split_hi(l, C_Q, 0)
                copy_out(Q_K + 1, 0, kT[:, 4:6, :])
                split_hi(l, C_Q, 1)
                copy_out(Q_K + 1, 1, kT[:, 6:8, :])
                split_hi(l, C_Q + 1, 0)
                split_hi(l, C_Q + 1, 1)
                split_hi(l, C_V, 0)

                def exp_scores(h):
                    act.wait_ge(s_nb, l * XH + h + 1)
                    for t in range(TT):
                        ins = act.activation(pr[:, h, t, :], mb[h % 2][:, t * TOK:(t + 1) * TOK], ACT.Exp,
                                             bias=nbias[:, h, t:t + 1], scale=r_16[:, t:t + 1],
                                             accum_out=rsum[:, h, t:t + 1])
                    ins.then_inc(s_mf[h % 2], 1)

                def head_hi(h):
                    q = Q_AV + h // 2
                    wait_pass(l, q, h % 2)
                    act.activation(xT_hi[:, 2 * h:2 * h + 2, :], acc[q % 2][h % 2][:, :], ACT.Copy).then_inc(s_ohi, 1)
                exp_scores(0)
                exp_scores(1)
                split_hi(l, C_V, 1)
                split_hi(l, C_V + 1, 0)
                copy_out(Q_V, 0, vx[:, 0, 0:COL])
                exp_scores(2)
                split_hi(l, C_V + 1, 1)
                copy_out(Q_V, 1, vx[:, 1, 0:COL])
                exp_scores(3)
                split_hi(l, C_O, 0)
                copy_out(Q_V + 1, 0, vx[:, 0, COL:2 * COL])
                split_hi(l, C_O, 1)
                copy_out(Q_V + 1, 1, vx[:, 1, COL:2 * COL])
                for h in range(XH):
                    head_hi(h)
                split_hi(l, C_O + 1, 0)
                y_square(l, 2, Q_O, 0, 0)
                split_hi(l, C_O + 1, 1)
                boundary(l, 2, Q_O + 1, C_O + 1)

            act.dma_start(pos_i[:, :], a["positions"]).then_inc(s_pos, 16)
            act.dma_start(inv_f[:, :], a["inv_freq"]).then_inc(s_pos, 16)
            act.wait_ge(s_setup, 11)
            act.activation(sin_t[:, :, :], rest[3][:, :, :], ACT.Sin).then_inc(s_trig, 1)
            act.activation(cos_t[:, :, :], carg[:, :, :], ACT.Sin).then_inc(s_trig, 1)
            act.wait_ge(s_first, 32)
            x_hi(0, 0, 0)
            for h in range(2):
                act.wait_ge(s_raw[h], 16)
                for k in range(4):
                    g = G_FFN1 * KD + 4 * h + k
                    act.activation(w_hi[:, h, k, :], raw[:, h, k, :], ACT.Copy,
                                   scale=gains[:, g:g + 1]).then_inc(s_hi, 1)
            x_square(0, 0, 0)
            split_hi(0, 1, 0)
            with act.Fori(0, LAYERS) as l:
                ffn(l, 0)
                mixer(l)
                mix_out(l)
                attention(l)
                ffn(l, 1)

        @block.vector
        def _(dve):
            def split_lo(l, ci, h, i=None):
                lay = l
                if ci >= N_CH:
                    lay = other(l)
                _, _, _, nk, gain = CHUNKS[ci % N_CH]
                slot = (2 * ci + h) % 4
                before = 4 * half_no(l, ci, h) + (0 if i is None else i * 16)
                if gain is None:
                    for a, b in pieces(nk):
                        dve.wait_ge(s_hi, before + a + 2)
                        dve.tensor_tensor(w_lo[:, slot, a:b, :], raw[:, slot, a:b, :],
                                          w_hi[:, slot, a:b, :].bitcast(F32), ALU.subtract).then_inc(s_lo, 2)
                    return
                for k in range(nk):
                    dve.wait_ge(s_hi, before + k + 1)
                    g = lay * (N_GAINS * KD) + gain * KD + h * nk + k
                    dve.scalar_tensor_tensor(w_lo[:, slot, k, :], raw[:, slot, k, :], gains[:, ds(g, 1)],
                                             w_hi[:, slot, k, :].bitcast(F32), ALU.mult,
                                             ALU.subtract).then_inc(s_lo, 1)

            def t_lo(l, use, dst, hi, extra_t=0, extra_s=0):
                dve.wait_ge(s_thi, ts_no(l, use) + 1 + extra_s)
                dve.tensor_tensor(dst, tb[t_bank(use)][:, :].rearrange("p (k n) -> p k n", k=dst.shape[1]),
                                  hi.bitcast(F32), ALU.subtract).then_inc(s_tev, 1)

            def t_copy(l, use, dst, rows=P, cols=COL):
                dve.wait_ge(s_t, t_no(l, use) + 1)
                src = tb[t_bank(use)][0:rows, 0:cols]
                if len(dst.shape) == 3:
                    src = src.rearrange("p (k n) -> p k n", k=dst.shape[1])
                dve.tensor_copy(dst, src).then_inc(s_tev, 1)

            def x_lo(l, phase, t):
                for g in range(2):
                    s = (slice(None), slice(4 * g, 4 * g + 4), slice(t * P, (t + 1) * P))
                    t_lo(l, ("x", phase, t, g), xT_lo[s], xT_hi[s])

            def y_gain(l, phase, q, n, t):
                if n == 0 and t == 0:
                    dve.wait_ge(s_gain, (l * 4 + phase + 1) * 16)
                dve.wait_ge(s_ysq, y_no(l, phase, n, t) + 1)
                dve.tensor_tensor(yg[:, t, n * COL:(n + 1) * COL], acc[q % 2][t][:, :],
                                  post_gain[:, n * COL:(n + 1) * COL], ALU.mult).then_inc(s_accf[bank(q, t)], 1)

            def x_update(l, phase, q, t):
                dve.wait_ge(s_rpost, l * 8 + 2 * phase + t + 1)
                dve.wait_ge(s_accf[bank(q, t)], acc_uses(l, q) + 1)
                for n in range(2):
                    s = slice(n * COL, (n + 1) * COL)
                    dve.scalar_tensor_tensor(x[:, t, s], yg[:, t, s], r_post[:, t:t + 1], x[:, t, s],
                                             ALU.mult, ALU.add).then_inc(s_x, 1)

            def boundary(l, phase, q, ci):
                y_gain(l, phase, q, 1, 0)
                x_update(l, phase, q, 0)
                split_lo(l, ci + 1, 0)
                x_lo(l, phase + 1, 0)
                if phase == 2:
                    y_gain(l, phase, q - 1, 0, 1)
                split_lo(l, ci + 1, 1)
                y_gain(l, phase, q, 1, 1)
                x_update(l, phase, q, 1)
                split_lo(l, ci + 2, 0)

            def ffn(l, f):
                c0, q0, phase = C_FFN[f], Q_FFN[f], (0, 3)[f]
                split_lo(l, c0 + 1, 1)
                x_lo(l, phase, 1)

                def h_lo(j, i):
                    if i is None:
                        s = (slice(None), slice(2 * j, 2 * j + 2), slice(None))
                    else:
                        s = (slice(None), ds(i * 4 + 2 * j, 2), slice(None))
                    t_lo(l, ("h", f, j), hT_lo[s], hT_hi[s], extra_s=0 if i is None else i * 2)

                def gated(j, t, i):
                    base = gated_no(l, f, j, t, i) + 1
                    b = acc[(q0 + j) % 2][t]
                    dve.wait_ge(s_tanh, base)
                    if j == 1:
                        dve.wait_ge(s_accf[bank(q0, t)], acc_uses(l, q0) + 1)
                    dve.scalar_tensor_tensor(gt[:, t, :], th[:, t, :], 1.0, b[:, 0:256], ALU.add,
                                             ALU.mult).then_inc(s_gated, 1)
                    dve.wait_ge(s_gated, base)
                    dve.scalar_tensor_tensor(h_tok[:, j % 2, t, :], gt[:, t, :], c_half[:, t:t + 1], b[:, 256:512],
                                             ALU.mult, ALU.mult).then_inc(s_accf[bank(q0 + j, t)], 1)

                def up(j, i=None):
                    gated(j, 0, i)
                    h_lo(j - 1, i)
                    split_lo(l, c0 + j + 1, 1, i)
                    gated(j, 1, i)
                    split_lo(l, c0 + j + 2, 0, i)
                gated(0, 0, None)
                gated(1, 0, None)
                split_lo(l, c0 + 2, 0)
                gated(0, 1, None)
                split_lo(l, c0 + 2, 1)
                gated(1, 1, None)
                h_lo(0, None)
                split_lo(l, c0 + 3, 0)
                with dve.Fori(0, (FU - 5) // 2) as i:
                    for p in range(2):
                        up(2 + p, i)
                for j in range(FU - 3, FU):
                    up(j)
                for d in range(6):
                    ci = c0 + FU + d
                    if d == 0:
                        h_lo(FU - 1, None)
                    if d == 3:
                        y_gain(l, phase, q0 + FU, 0, 0)
                        y_gain(l, phase, q0 + FU, 0, 1)
                    if d < 5:
                        split_lo(l, ci + 1, 1)
                    if d < 4:
                        split_lo(l, ci + 2, 0)
                boundary(l, phase, q0 + FU + 1, c0 + FU + 5)

            def mixer(l):
                def split_after(k):
                    ci = C_IN + k // 2
                    if k % 2 == 0:
                        split_lo(l, ci + 1, 1)
                    else:
                        split_lo(l, ci + 2, 0)

                def level_out(n):
                    b = LEVELS[n]
                    for e in range(2):
                        dve.wait_ge(s_m[e], m_no(l, f"lv{n}") + 1)
                        if b == P:
                            dve.tensor_copy(pgx[:, e].rearrange("p r i -> p (r i)"),
                                            mb[e][:, 0:2 * P]).then_inc(s_mf[e], 1)
                            continue
                        dve.wait_ge(s_mf[e], m_no(l, f"lv{n}"))
                        dst = pg[:, e].rearrange("p c (g two b) -> p c g two b", two=2, b=b)[:, :, :, 1, :]
                        src = mb[e][:, 0:4 * 64].rearrange("p (c g b) -> p c g b", c=4, b=b)
                        msk = lv_mask[:, n - 1, :].rearrange("p (g b) -> p g b", b=b)
                        msk = msk.unsqueeze(1).to_broadcast([P, 4, 64 // b, b])
                        dve.nop(nofuse=True)
                        dve.copy_predicated(dst, msk, src).then_inc(s_mf[e], 1)

                def retention_mask(j):
                    for e in range(2):
                        dve.wait_ge(s_m[e], m_no(l, f"rj{j}") + 1)
                        w = TOK if j == 0 else P
                        dst = (pr0, pr1)[j][:, e]
                        dve.tensor_tensor(dst, mb[e][:, 0:2 * w].rearrange("p (r i) -> p r i", r=2),
                                          decay[:, e, :, 0:w], ALU.mult).then_inc(s_mf[e], 1)

                def head_squares(use, g):
                    for t in range(TT):
                        dve.wait_ge(s_mf[t], m_no(l, use) + 1)
                        sq = (rot_a, rot_b)[t]
                        dve.tensor_reduce(hss[:, t, 4 * g:4 * g + 4], sq[:, :].rearrange("p (h d) -> p h d", h=HEADS),
                                          AX.X, ALU.add).then_inc(s_hss, 1)

                def gate_z(c, t):
                    g = c - 4
                    dve.wait_ge(s_gtanh, l * 4 + 2 * g + t + 1)
                    s = gate[:, t, g * COL:(g + 1) * COL]
                    dve.scalar_tensor_tensor(s, s, 1.0, acc[(Q_IN + c) % 2][t][:, :], ALU.add,
                                             ALU.mult).then_inc(s_accf[bank(Q_IN + c, t)], 1)

                def mixed(c, t):
                    g = c - 4
                    q = Q_IN + c
                    dve.wait_ge(s_accf[bank(q, t)], acc_uses(l, q) + 1)
                    dve.wait_ge(s_of, l * 4 + 2 * g + t + 1)
                    s = (slice(None), t, slice(g * COL, (g + 1) * COL))
                    dve.tensor_tensor(o_sb[s], o_sb[s], gate[s], ALU.mult).then_inc(s_mixed, 1)

                g_mix = gains[:, ds(l * (N_GAINS * KD) + G_MIX * KD, KD)].unsqueeze(2).to_broadcast([P, KD, RANK])
                dve.tensor_tensor(w_ga_s[:, :, :], w_ga[:, ds(l, 1), :, :].rearrange("p o k n -> p (o k) n"), g_mix,
                                  ALU.mult).then_inc(s_gas, 1)
                split_lo(l, C_IN + 1, 1)
                x_lo(l, 1, 1)
                dve.wait_ge(s_gah, l + 1)
                dve.tensor_tensor(w_ga_lo[:, :, :], w_ga_s[:, :, :], w_ga_hi[:, :, :].bitcast(F32),
                                  ALU.subtract).then_inc(s_gal, 1)
                split_lo(l, C_IN + 2, 0)
                dve.wait_ge(s_m[0], m_no(l, "z") + 1)
                dve.tensor_copy(r_row, mb[0][0:RANK, TOK:2 * TOK]).then_inc(s_rrow, 1)
                dve.wait_ge(s_rrow, l + 1)
                dve.tensor_tensor(gaT[:, :], mb[0][0:RANK, 0:TOK], r_row, ALU.mult).then_inc(s_mf[0], 1)
                split_lo(l, C_IN + 2, 1)
                dve.wait_ge(s_m[1], m_no(l, "z") + 1)
                dve.tensor_tensor(zb, mb[1][:, :].rearrange("p (r i) -> p r i", r=2),
                                  b_a2[:, ds(l * 2, 2)].unsqueeze(2).to_broadcast([P, 2, TOK]),
                                  ALU.add).then_inc(s_mf[1], 1)
                for t in range(TT):
                    t_copy(l, ("gqk", t), gT[:, :, t * P:(t + 1) * P])
                dve.wait_ge(s_lsig, l * 3 + 3)
                dve.scalar_tensor_tensor(zb, zb, 0.0, lg, ALU.min, ALU.subtract).then_inc(s_la, 1)
                dve.wait_ge(s_la, l + 1)
                for r in range(2):
                    for t in range(TT):
                        tile = slice(t * P, (t + 1) * P)
                        dve.tensor_tensor_scan(cum[:, r, tile], ones[:, :], zb[:, r, tile], 0.0,
                                               ALU.mult, ALU.add).then_inc(s_cum, 1)
                for e in range(2):
                    dve.wait_ge(s_m[e], m_no(l, "diag") + 1)
                    dve.tensor_tensor(pg[:, e], mb[e][:, :].rearrange("p (c i) -> p c i", c=4),
                                      ident[:, :].unsqueeze(1).to_broadcast([P, 4, P]), ALU.mult).then_inc(s_mf[e], 1)
                split_after(3)
                split_after(4)
                level_out(0)
                level_out(1)
                for t in range(TT):
                    t_copy(l, ("rqk", t), rT[:, :, t * P:(t + 1) * P])
                split_after(5)
                level_out(2)
                split_after(6)
                retention_mask(0)
                level_out(3)
                split_after(7)
                retention_mask(1)
                gate_z(4, 0)
                level_out(4)
                level_out(5)
                split_after(8)
                head_squares("ro", 0)
                gate_z(4, 1)
                level_out(6)
                level_out(7)
                split_after(9)
                head_squares("go", 1)
                for t in range(TT):
                    mixed(4, t)
                gate_z(5, 0)
                mixed(5, 0)
                split_after(10)

                def mix_lo(t):
                    for g in range(2):
                        s = (slice(None), slice(4 * g, 4 * g + 4), slice(t * P, (t + 1) * P))
                        t_lo(l, ("mix", t, g), xT_lo[s], xT_hi[s])
                mix_lo(0)
                gate_z(5, 1)
                mixed(5, 1)
                split_after(11)
                mix_lo(1)
                split_lo(l, C_OUT + 1, 1)

            def mem_lo(l, t):
                for g in range(2):
                    s = (slice(None), slice(4 * g, 4 * g + 4), slice(t * P, (t + 1) * P))
                    t_lo(l, ("mem", t, g), mT_lo[s], mT_hi[s])

            def mix_out(l):
                for t in range(TT):
                    dve.wait_ge(s_rmem, l * 2 + t + 1)
                    dve.tensor_scalar(mem_t[:, t, :], mem_t[:, t, :], r_mem[:, t:t + 1], None,
                                      ALU.mult).then_inc(s_memn, 1)
                y_gain(l, 1, Q_OUT, 0, 0)
                mem_lo(l, 0)
                y_gain(l, 1, Q_OUT + 1, 1, 0)
                x_update(l, 1, Q_OUT + 1, 0)
                split_lo(l, C_OUT + 2, 0)
                mem_lo(l, 1)
                y_gain(l, 1, Q_OUT, 0, 1)
                split_lo(l, C_OUT + 2, 1)
                y_gain(l, 1, Q_OUT + 1, 1, 1)
                x_update(l, 1, Q_OUT + 1, 1)
                split_lo(l, C_K + 1, 0)

            def attention(l):
                x_lo(l, 2, 0)
                split_lo(l, C_K + 1, 1)
                x_lo(l, 2, 1)
                split_lo(l, C_Q, 0)
                split_lo(l, C_Q, 1)
                split_lo(l, C_Q + 1, 0)

                def q_copy(c, t):
                    q = Q_Q + c
                    dve.wait_ge(s_acc, pass_no(l, q, t) + 1)
                    dve.tensor_copy(qT[:, 4 * c + 2 * t:4 * c + 2 * t + 2, :].rearrange("p k i -> p (k i)"),
                                    acc[q % 2][t][:, :]).then_inc(s_accf[bank(q, t)], 1)

                def m_use(h):
                    return m_no(l, "s0" if h < 2 else "s1")

                def bias(h):
                    dve.wait_ge(s_m[h % 2], m_use(h) + 1)
                    dve.tensor_reduce(smax[:, h, :], mb[h % 2][:, :].rearrange("p (t m) -> p t m", t=TT), AX.X,
                                      ALU.max).then_inc(s_smax, 1)
                    dve.wait_ge(s_smax, l * XH + h + 1)
                    dve.wait_ge(s_rpre, l * 8 + 2 * 2 + 1 + 1)
                    dve.tensor_tensor(nbias[:, h, :], smax[:, h, :], n_16[:, :], ALU.mult).then_inc(s_nb, 1)

                def normalise(h):
                    dve.wait_ge(s_mf[h % 2], m_use(h) + 1)
                    dve.reciprocal(rinv[:, h, :], rsum[:, h, :]).then_inc(s_rinv, 1)
                    dve.wait_ge(s_rinv, l * XH + h + 1)
                    for t in range(TT):
                        ins = dve.tensor_scalar(pr[:, h, t, :], pr[:, h, t, :], rinv[:, h, t:t + 1], None,
                                                ALU.mult)
                    ins.then_inc(s_p, 1)

                def p_copy(h):
                    t_copy(l, ("p", h), pT[h])

                def head_lo(h):
                    q = Q_AV + h // 2
                    dve.wait_ge(s_ohi, l * XH + h + 1)
                    s = (slice(None), slice(2 * h, 2 * h + 2), slice(None))
                    dve.tensor_tensor(xT_lo[s], acc[q % 2][h % 2][:, :].rearrange("p (k i) -> p k i", k=2),
                                      xT_hi[s].bitcast(F32), ALU.subtract).then_inc(s_accf[bank(q, h % 2)], 1)
                q_copy(0, 0)
                split_lo(l, C_Q + 1, 1)
                q_copy(0, 1)
                split_lo(l, C_V, 0)
                q_copy(1, 0)
                bias(0)
                bias(1)
                split_lo(l, C_V, 1)
                normalise(0)
                q_copy(1, 1)
                split_lo(l, C_V + 1, 0)
                normalise(1)
                bias(2)
                split_lo(l, C_V + 1, 1)
                bias(3)
                normalise(2)
                p_copy(0)
                p_copy(1)
                split_lo(l, C_O, 0)
                normalise(3)
                p_copy(2)
                split_lo(l, C_O, 1)
                p_copy(3)
                for h in range(XH):
                    head_lo(h)
                split_lo(l, C_O + 1, 0)
                y_gain(l, 2, Q_O, 0, 0)
                split_lo(l, C_O + 1, 1)
                boundary(l, 2, Q_O + 1, C_O + 1)

            dve.memset(ones[:, :], 1.0)
            dve.wait_ge(s_pos, 32)
            n_set = [0]

            def setup(ins):
                n_set[0] += 1
                ins.then_inc(s_setup, 1)
                dve.wait_ge(s_setup, n_set[0])

            def flat(t):
                return t[:, :, :].rearrange("p t f -> p (t f)")
            two_pi = 2.0 * np.pi
            c1 = 6.28125
            c2 = float(np.float32(np.round((two_pi - c1) * 2 ** 21) / 2 ** 21))
            c3 = float(two_pi - c1 - c2)
            magic = 1.5 * 2.0 ** 23
            setup(dve.tensor_copy(pos_f[:, :], pos_i[:, :]))
            setup(dve.tensor_tensor(ang[:, :, :], pos_f[:, :].unsqueeze(2).to_broadcast([P, TT, 32]),
                                    inv_f[:, :].unsqueeze(1).to_broadcast([P, TT, 32]), ALU.mult))
            setup(dve.tensor_scalar(flat(turns), flat(ang), 1.0 / two_pi, None, ALU.mult))
            setup(dve.tensor_scalar(flat(turns), flat(turns), magic, None, ALU.add))
            setup(dve.tensor_scalar(flat(turns), flat(turns), -magic, None, ALU.add))
            setup(dve.scalar_tensor_tensor(flat(rest[0]), flat(turns), -c1, flat(ang), ALU.mult, ALU.add))
            setup(dve.scalar_tensor_tensor(flat(rest[1]), flat(turns), -c2, flat(rest[0]), ALU.mult, ALU.add))
            setup(dve.scalar_tensor_tensor(flat(rest[2]), flat(turns), -c3, flat(rest[1]), ALU.mult, ALU.add))
            setup(dve.tensor_scalar(flat(rest[3]), flat(rest[2]), 3.1415925, -3.1415925, ALU.min, ALU.max))
            setup(dve.scalar_tensor_tensor(flat(absr), flat(rest[3]), -1.0, flat(rest[3]), ALU.mult, ALU.max))
            setup(dve.tensor_scalar(flat(carg), flat(absr), -1.0, float(np.pi / 2), ALU.mult, ALU.add))
            dve.wait_ge(s_trig, 2)
            dve.tensor_copy(rope_c[:, :, 0:32], cos_t[:, :, :])
            dve.tensor_copy(rope_c[:, :, 32:64], cos_t[:, :, :])
            dve.tensor_scalar(rope_s[:, :, 0:32], sin_t[:, :, :], -1.0, None, ALU.mult)
            dve.tensor_copy(rope_s[:, :, 32:64], sin_t[:, :, :]).then_inc(s_rope_t, 1)
            dve.wait_ge(s_first, 32)
            x_lo(0, 0, 0)
            for h in range(2):
                for k in range(4):
                    dve.wait_ge(s_hi, 4 * h + k + 1)
                    g = G_FFN1 * KD + 4 * h + k
                    dve.scalar_tensor_tensor(w_lo[:, h, k, :], raw[:, h, k, :], gains[:, g:g + 1],
                                             w_hi[:, h, k, :].bitcast(F32), ALU.mult, ALU.subtract).then_inc(s_lo, 1)
            split_lo(0, 1, 0)
            dve.wait_ge(s_const, 16 * 5)
            with dve.Fori(0, LAYERS) as l:
                ffn(l, 0)
                mixer(l)
                mix_out(l)
                attention(l)
                ffn(l, 1)

        @block.gpsimd
        def _(pool):
            class Steps:

                def __init__(self, start, per_layer):
                    self.start, self.per_layer, self.n, self.l = start, per_layer, 0, 0

                def value(self):
                    return self.start + self.l * self.per_layer + self.n

                def layer(self, l):
                    self.l, self.n = l, 0

            steps = Steps(1, POOL_STEPS)

            def then(ins):
                ins.then_inc(s_pool, 1)
                steps.n += 1
                pool.wait_ge(s_pool, steps.value())

            def post(l, phase, t):
                scale = 4.0 if phase in (0, 3) else 1.0
                pool.wait_ge(s_ysq, y_no(l, phase, 1, t) + 1)
                c = slice(t, t + 1)
                then(pool.tensor_tensor(v_post[:, c], yss[:, t, 0:1], yss[:, t, 1:2], ALU.add))
                pool.nop(nofuse=True)
                then(pool.tensor_scalar(v_post[:, c], v_post[:, c], scale / D, scale * EPS, ALU.mult, ALU.add))
                pool.tensor_tensor(r_post[:, c], v_post[:, c], half_neg[:, 0:1], ALU.pow).then_inc(s_rpost, 1)

            def pre(l, phase, t):
                pool.wait_ge(s_xsq, l * 8 + 2 * phase + t + 1)
                c = slice(t, t + 1)
                pool.nop(nofuse=True)
                then(pool.tensor_scalar(v_pre[:, c], xss[:, c], 1.0 / D, EPS, ALU.mult, ALU.add))
                then(pool.tensor_tensor(r_pre[:, c], v_pre[:, c], half_neg[:, 0:1], ALU.pow))
                pool.nop(nofuse=True)
                pool.tensor_scalar(r_8[:, c], r_pre[:, c], DK ** -0.5, 0.0, ALU.mult, ALU.add)
                pool.tensor_scalar(r_16[:, c], r_pre[:, c], 1.0 / 16, 0.0, ALU.mult, ALU.add)
                pool.tensor_scalar(n_16[:, c], r_pre[:, c], -1.0 / 16, 0.0, ALU.mult, ALU.add)
                then(pool.tensor_scalar(r_half[:, c], r_pre[:, c], 0.5, 0.0, ALU.mult, ALU.add))
                pool.tensor_tensor(c_half[:, c], r_half[:, c], r_pre[:, c], ALU.mult).then_inc(s_rpre, 1)

            def rope(l, t):
                q = Q_IN + 1
                pool.wait_ge(s_accf[bank(q, t)], acc_uses(l, q) + 1)
                if t == 1:
                    pool.wait_ge(s_rope, l * 2 + 1)
                z = rqk[:, t, :].rearrange("p (h d) -> p h d", h=8)
                ra = rot_a[:, :].rearrange("p (h d) -> p h d", h=8)
                rb = rot_b[:, :].rearrange("p (h d) -> p h d", h=8)
                pool.tensor_tensor(ra, z, rope_c[:, t, :].unsqueeze(1).to_broadcast([P, 8, DK]), ALU.mult)
                for half in range(2):
                    o, i = slice(32 * half, 32 * half + 32), slice(32 - 32 * half, 64 - 32 * half)
                    ins = pool.tensor_tensor(rb[:, :, o], z[:, :, i],
                                             rope_s[:, t, o].unsqueeze(1).to_broadcast([P, 8, 32]), ALU.mult)
                then(ins)
                pool.tensor_tensor(rqk[:, t, :], rot_a[:, :], rot_b[:, :], ALU.add).then_inc(s_rope, 1)

            def blocks(ap, b):
                return ap.rearrange("p (g two b) -> p g two b", two=2, b=b)

            def exponents(l, n):
                b = LEVELS[n]
                if n >= 2:
                    pool.wait_ge(s_av, l * 8 + n - 1)
                e = dec[n % 2]
                if b == P:
                    e3 = e.rearrange("p (r i) -> p r i", r=2)
                    pool.tensor_tensor(e3[:, :, 0:P], cum[:, :, P - 1:P].to_broadcast([P, 2, P]), cum[:, :, 0:P],
                                       ALU.subtract)
                    pool.tensor_copy(e3[:, :, P:2 * P], cum[:, :, P:2 * P]).then_inc(s_tmp, 1)
                    return
                eb, cb = blocks(e, b), blocks(cum[:, :, :].rearrange("p r i -> p (r i)"), b)
                ref = cb[:, :, 0, b - 1:b].to_broadcast([P, 256 // b, b])
                pool.tensor_tensor(eb[:, :, 0, :], ref, cb[:, :, 0, :], ALU.subtract)
                pool.tensor_tensor(eb[:, :, 1, :], cb[:, :, 1, :], ref, ALU.subtract).then_inc(s_tmp, 1)

            def decayed(l, n):
                b = LEVELS[n]
                pool.wait_ge(s_dec, l * 8 + n + 1)
                if n >= 2:
                    pool.wait_ge(s_m[1], m_no(l, f"lv{n - 2}") + 1)
                o, d = blocks(av[n % 2], b), blocks(dec[n % 2], b)
                k = blocks(gT[:, 2:4, :].rearrange("p r i -> p (r i)"), b)
                q = blocks(gT[:, 0:2, :].rearrange("p r i -> p (r i)"), b)
                pool.tensor_tensor(o[:, :, 0, :], k[:, :, 0, :], d[:, :, 0, :], ALU.mult)
                pool.tensor_tensor(o[:, :, 1, :], q[:, :, 1, :], d[:, :, 1, :], ALU.mult).then_inc(s_av, 1)

            def heads(l, g):
                pool.wait_ge(s_hss, l * 4 + 2 * g + 2)
                s = (slice(None), slice(None), slice(4 * g, 4 * g + 4))
                hn = half_neg[:, :].rearrange("p (t h) -> p t h", t=TT)
                pool.nop(nofuse=True)
                then(pool.tensor_scalar(v_head[s], hss[s], 1.0 / DV, EPS, ALU.mult, ALU.add))
                then(pool.tensor_tensor(r_head[s], v_head[s], hn, ALU.pow))
                then(pool.tensor_tensor(f_head[s], r_head[s], r_half[:, :].unsqueeze(2).to_broadcast([P, TT, 4]),
                                        ALU.mult))
                for t in range(TT):
                    o = o_sb[:, t, g * COL:(g + 1) * COL].rearrange("p (h d) -> p h d", h=HEADS)
                    pool.tensor_tensor(o, o, f_head[:, t, 4 * g:4 * g + 4].unsqueeze(2).to_broadcast([P, HEADS, DV]),
                                       ALU.mult).then_inc(s_of, 1)

            def mem_norm(l, t):
                pool.wait_ge(s_msq, l * 2 + t + 1)
                c = slice(t, t + 1)
                pool.nop(nofuse=True)
                then(pool.tensor_scalar(v_mem[:, c], mss[:, c], 1.0 / D, EPS, ALU.mult, ALU.add))
                pool.tensor_tensor(r_mem[:, c], v_mem[:, c], half_neg[:, 0:1], ALU.pow).then_inc(s_rmem, 1)

            def mixer(l):
                pre(l, 1, 1)
                pool.tensor_copy(w_a2_l[:, :], w_a2[:, ds(l, 1), :].rearrange("r o n -> r (o n)")).then_inc(s_a2, 1)
                rope(l, 0)
                rope(l, 1)
                pool.wait_ge(s_cum, l * 4 + 4)
                pool.wait_ge(s_tev, t_no(l, ("gqk", 1)) + 1)
                exponents(l, 0)
                exponents(l, 1)
                for n in range(8):
                    decayed(l, n)
                    if n + 2 < 8:
                        exponents(l, n + 2)
                heads(l, 0)
                heads(l, 1)

            for count in (s_acc, s_half, *s_accf, *s_m, *s_mf):
                pool.sem_inc(count, 1)
            pool.memset(half_neg[:, :], -0.5).then_inc(s_pool, 1)
            pool.wait_ge(s_pool, 1)
            steps.start = 1
            for t in range(TT):
                pool.wait_ge(s_x_in[t], 16)
                pool.sem_inc(s_x, 2)
            pre(0, 0, 0)
            steps.start += steps.n
            pool.wait_ge(s_const, 16 * 5)
            pool.wait_ge(s_rope_t, 1)
            with pool.Fori(0, LAYERS) as l:
                steps.layer(l)
                pre(l, 0, 1)
                post(l, 0, 0)
                pre(l, 1, 0)
                post(l, 0, 1)
                mixer(l)
                for t in range(TT):
                    mem_norm(l, t)
                post(l, 1, 0)
                pre(l, 2, 0)
                post(l, 1, 1)
                pre(l, 2, 1)
                post(l, 2, 0)
                pre(l, 3, 0)
                post(l, 2, 1)
                pre(l, 3, 1)
                post(l, 3, 0)
                pre(l, 4, 0)
                post(l, 3, 1)
                assert steps.n == POOL_STEPS, steps.n


def constants():
    gamma_log = np.log1p(-np.exp2(-5.0 - np.arange(HEADS)))
    j, i = np.arange(P)[:, None], np.arange(TOK)[None, :]
    decay = np.zeros((P, 2, 2, TOK))
    for h in range(HEADS):
        power = np.exp(np.where(i >= j, i - j, 0) * gamma_log[h])
        decay[:, h % 2, h // 2, :] = np.where(i >= j, power, 0.0) * DK ** -0.5
    mask = np.zeros((P, 7, 64), np.int8)
    for v, b in enumerate(LEVELS[1:]):
        for n in range(64):
            first = 2 * b * (n // b)
            mask[first:first + b, v, n] = 1
    inv_freq = 10000.0 ** (-np.arange(0, DK, 2, dtype=np.float64) / DK)
    return {
        "ident": np.eye(P, dtype=np.float32),
        "decay": decay.reshape(P, -1).astype(np.float32),
        "lv_mask": mask.reshape(P, -1).view(np.int32),
        "inv_freq": np.tile(inv_freq.astype(np.float32)[None, :], (P, 1)),
    }


def layouts(i):
    def rows(w):
        lay, k, n = w.shape
        w = w.reshape(lay, k // P, P, n // COL, COL).transpose(0, 3, 2, 1, 4)
        return np.ascontiguousarray(w).reshape(lay, n // COL, P, k // P * COL)

    def gate_up(g, u):
        def half(w):
            return w.reshape(LAYERS, KD, P, FU, 256).transpose(0, 3, 2, 1, 4)
        return np.concatenate([half(g), half(u)], axis=-1).reshape(LAYERS, FU, P, KD * COL)

    w = i["w_in"]
    rq, rk, rv, rg, gq, gk, gv, ga, gg = np.split(w, np.cumsum([256, 256, 512, 512, 256, 256, 512, 16]), axis=-1)
    by_row = [i["ffn1_pre_g"], i["mix_pre_g"], i["xa_mem_g"], i["xa_pre_g"], i["ffn2_pre_g"],
              np.concatenate([i["ret_norm_g"], i["gla_norm_g"]], axis=1).reshape(LAYERS, D)]
    gains = np.stack(by_row, axis=1).reshape(LAYERS, N_GAINS, KD, P).transpose(3, 0, 1, 2)
    post = np.stack([i["ffn1_post_g"], i["mix_post_g"], i["xa_post_g"], i["ffn2_post_g"]], axis=1)
    arrays = {
        "x": i["x"].reshape(TOK, D), "mem": i["mem"].reshape(TOK, D),
        "positions": i["positions"].reshape(TT, P).T,
        "gu0": gate_up(i["ffn1_w_gate"], i["ffn1_w_up"]), "down0": rows(i["ffn1_w_down"]),
        "gu1": gate_up(i["ffn2_w_gate"], i["ffn2_w_up"]), "down1": rows(i["ffn2_w_down"]),
        "in": rows(np.concatenate([gq, gk, rq, rk, gv, rv, rg, gg], axis=-1)),
        "out": rows(i["w_out"]), "kv": rows(i["xa_w_kv"]), "q": rows(i["xa_w_q"]), "o": rows(i["xa_w_o"]),
        "w_ga": ga.reshape(LAYERS, KD, P, RANK).transpose(2, 0, 1, 3).reshape(P, -1),
        "w_a2": i["w_a2"].transpose(1, 0, 2).reshape(RANK, -1),
        "b_a2": i["b_a2"].reshape(LAYERS, 2, P).transpose(2, 0, 1).reshape(P, -1),
        "gains": gains.reshape(P, -1), "post_g": post.reshape(LAYERS * 4, D),
    }
    return {**arrays, **constants()}


def kernel(**inputs):
    import concourse.bacc as bacc
    from concourse.bass_utils import run_bass_kernel_spmd

    nc = bacc.Bacc("TRN2", target_bir_lowering=False, num_devices=1)
    arrays, aps = {}, {}
    for name, arr in layouts({k: np.asarray(v) for k, v in inputs.items()}).items():
        arrays[f"in_{name}"] = np.ascontiguousarray(arr)
        aps[name] = nc.dram_tensor(f"in_{name}", arr.shape, mybir.dt.from_np(arr.dtype), kind="ExternalInput").ap()
    out = nc.dram_tensor("out", (TOK, D), F32, kind="ExternalOutput").ap()
    program(nc, aps, out)
    r = run_bass_kernel_spmd(nc, [arrays], core_ids=[0])
    return r.results[0]["out"].reshape(1, TOK, D)
```
